# Optimizing a Trainium2 kernel written in Bass

```python
import math
import jax
import jax.numpy as jnp
from jax import lax
import numpy as np

D_MODEL = 1024
BATCH = 1
SEQ = 256
DEPTH = 2

MEM_LEN = 256
POOL_WIDTH = D_MODEL // 2
POOL_GROUPS = 4
POOL_WINDOWS = (2, 4, 8, 16)
POOL_GROUP_IN = POOL_WIDTH // POOL_GROUPS
POOL_GROUP_OUT = D_MODEL // POOL_GROUPS
CONV_WIDTH = D_MODEL // 2
CONV_KERNEL = 31
IN_COLS = POOL_WIDTH + 2 * CONV_WIDTH + 2 * D_MODEL
N_XHEADS = 4
XHEAD_DIM = D_MODEL // N_XHEADS
D_FF = 2816
N_EXPERTS = 8
TOP_K = 2
N_DENSE = (DEPTH + 1) // 2
N_MOE = DEPTH // 2
EPS = 1e-6

kernel_name = "hybrid_pool_conformer_xattn_moe_trunk"

def rmsnorm(x, g):
    xf = x.astype(jnp.float32)
    y = xf * lax.rsqrt(jnp.mean(xf * xf, axis=-1, keepdims=True) + EPS)
    return (y * g.astype(jnp.float32)).astype(x.dtype)

def layernorm(x, g, b):
    xf = x.astype(jnp.float32)
    mu = jnp.mean(xf, axis=-1, keepdims=True)
    var = jnp.mean(jnp.square(xf - mu), axis=-1, keepdims=True)
    y = (xf - mu) * lax.rsqrt(var + EPS)
    return (y * g.astype(jnp.float32) + b.astype(jnp.float32)).astype(x.dtype)

def causal_multiscale_pool(u, w_pool, pool_scale):
    B, S, _ = u.shape
    ug = u.reshape(B, S, POOL_GROUPS, POOL_GROUP_IN).astype(jnp.float32)
    cs = jnp.cumsum(ug, axis=1)
    t = jnp.arange(1, S + 1, dtype=jnp.float32)
    outs = []
    for g, w in enumerate(POOL_WINDOWS):
        c = cs[:, :, g]
        lag = jnp.pad(c, ((0, 0), (w, 0), (0, 0)))[:, :S]
        cnt = jnp.minimum(t, float(w))[None, :, None]
        outs.append((c - lag) / cnt - ug[:, :, g])
    pooled = jnp.stack(outs, axis=2).astype(u.dtype)
    y = jnp.einsum('bsgc,gcd->bsgd', pooled, w_pool)
    return y.reshape(B, S, D_MODEL) * pool_scale

def conformer_conv(v, w_dw, b_dw, ln_g, ln_b, w_pw):
    a, b = jnp.split(v, 2, axis=-1)
    u = a * jax.nn.sigmoid(b)
    u = lax.conv_general_dilated(
        u, w_dw, window_strides=(1,), padding=[(CONV_KERNEL - 1, 0)],
        dimension_numbers=('NWC', 'WIO', 'NWC'),
        feature_group_count=CONV_WIDTH) + b_dw
    u = jax.nn.silu(layernorm(u, ln_g, ln_b))
    return u @ w_pw

def memory_cross_attention(h, m, w_q, w_kv, w_o):
    B, S, _ = h.shape
    M = m.shape[1]
    q = (h @ w_q).reshape(B, S, N_XHEADS, XHEAD_DIM)
    k, v = jnp.split(m @ w_kv, 2, axis=-1)
    k = k.reshape(B, M, N_XHEADS, XHEAD_DIM)
    v = v.reshape(B, M, N_XHEADS, XHEAD_DIM)
    s = jnp.einsum('bshd,bmhd->bhsm', q, k).astype(jnp.float32) * (XHEAD_DIM ** -0.5)
    p = jax.nn.softmax(s, axis=-1).astype(v.dtype)
    o = jnp.einsum('bhsm,bmhd->bshd', p, v).reshape(B, S, D_MODEL)
    return o @ w_o

def swiglu(h, w_gu, w_down):
    g, u = jnp.split(h @ w_gu, 2, axis=-1)
    return (jax.nn.silu(g) * u) @ w_down

def moe_swiglu(h, w_router, b_router, w_gu, w_down):
    B, S, D = h.shape
    tok = h.reshape(B * S, D)
    logits = tok.astype(jnp.float32) @ w_router.astype(jnp.float32) + b_router.astype(jnp.float32)
    top_v, top_i = lax.top_k(logits, TOP_K)
    gates = jax.nn.softmax(top_v, axis=-1)
    combine = jnp.sum(jax.nn.one_hot(top_i, N_EXPERTS, dtype=jnp.float32) * gates[..., None], axis=1)
    out = jnp.zeros((B * S, D), jnp.float32)
    for e in range(N_EXPERTS):
        out = out + combine[:, e:e + 1] * swiglu(tok, w_gu[e], w_down[e]).astype(jnp.float32)
    return out.reshape(B, S, D).astype(h.dtype)

def setup_inputs(seed: int = 0) -> dict:
    key = jax.random.key(seed)
    ks = iter(jax.random.split(key, 32))
    f32 = jnp.float32

    def w(shape, fan_in):
        return jax.random.normal(next(ks), shape, f32) * (fan_in ** -0.5)

    def gain(shape):
        return 1.0 + 0.01 * jax.random.normal(next(ks), shape, f32)

    def bias(shape):
        return 0.01 * jax.random.normal(next(ks), shape, f32)

    return {
        "x": jax.random.normal(next(ks), (BATCH, SEQ, D_MODEL), f32),
        "mem": jax.random.normal(next(ks), (BATCH, MEM_LEN, D_MODEL), f32),
        "g_mix": gain((DEPTH, D_MODEL)),
        "w_in": w((DEPTH, D_MODEL, IN_COLS), D_MODEL),
        "w_pool": w((DEPTH, POOL_GROUPS, POOL_GROUP_IN, POOL_GROUP_OUT), POOL_GROUP_IN),
        "pool_scale": 1.0 + 0.02 * jax.random.normal(next(ks), (DEPTH, D_MODEL), f32),
        "w_dw": w((DEPTH, CONV_KERNEL, 1, CONV_WIDTH), CONV_KERNEL),
        "b_dw": bias((DEPTH, CONV_WIDTH)),
        "conv_ln_g": gain((DEPTH, CONV_WIDTH)),
        "conv_ln_b": bias((DEPTH, CONV_WIDTH)),
        "w_conv_out": w((DEPTH, CONV_WIDTH, D_MODEL), CONV_WIDTH),
        "w_mix_out": w((DEPTH, D_MODEL, D_MODEL), D_MODEL),
        "g_xattn": gain((DEPTH, D_MODEL)),
        "g_mem": gain((DEPTH, D_MODEL)),
        "w_xq": w((DEPTH, D_MODEL, D_MODEL), D_MODEL),
        "w_xkv": w((DEPTH, D_MODEL, 2 * D_MODEL), D_MODEL),
        "w_xo": w((DEPTH, D_MODEL, D_MODEL), D_MODEL),
        "g_ffn": gain((DEPTH, D_MODEL)),
        "w_ffn_gu": w((N_DENSE, D_MODEL, 2 * D_FF), D_MODEL),
        "w_ffn_down": w((N_DENSE, D_FF, D_MODEL), D_FF),
        "w_router": w((N_MOE, D_MODEL, N_EXPERTS), D_MODEL),
        "b_router": bias((N_MOE, N_EXPERTS)),
        "w_moe_gu": w((N_MOE, N_EXPERTS, D_MODEL, 2 * D_FF), D_MODEL),
        "w_moe_down": w((N_MOE, N_EXPERTS, D_FF, D_MODEL), D_FF),
        "g_final": gain((D_MODEL,)),
    }

def reference(x, mem, g_mix, w_in, w_pool, pool_scale, w_dw, b_dw, conv_ln_g, conv_ln_b,
              w_conv_out, w_mix_out, g_xattn, g_mem, w_xq, w_xkv, w_xo, g_ffn,
              w_ffn_gu, w_ffn_down, w_router, b_router, w_moe_gu, w_moe_down, g_final):
    split_at = [POOL_WIDTH, POOL_WIDTH + 2 * CONV_WIDTH]
    for i in range(DEPTH):
        h = rmsnorm(x, g_mix[i])
        u_pool, v_conv, gate_logits = jnp.split(h @ w_in[i], split_at, axis=-1)
        gate_pool, gate_conv = jnp.split(jax.nn.sigmoid(gate_logits), 2, axis=-1)
        y_pool = causal_multiscale_pool(u_pool, w_pool[i], pool_scale[i])
        y_conv = conformer_conv(v_conv, w_dw[i], b_dw[i], conv_ln_g[i], conv_ln_b[i], w_conv_out[i])
        x = x + (gate_pool * y_pool + gate_conv * y_conv) @ w_mix_out[i]
        h = rmsnorm(x, g_xattn[i])
        m = rmsnorm(mem, g_mem[i])
        x = x + memory_cross_attention(h, m, w_xq[i], w_xkv[i], w_xo[i])
        h = rmsnorm(x, g_ffn[i])
        if i % 2 == 0:
            x = x + swiglu(h, w_ffn_gu[i // 2], w_ffn_down[i // 2])
        else:
            x = x + moe_swiglu(h, w_router[i // 2], b_router[i // 2], w_moe_gu[i // 2], w_moe_down[i // 2])
    return rmsnorm(x, g_final)


_drawn_inputs = setup_inputs


def setup_inputs(seed=0):
    import zlib

    import numpy as np

    out = dict(_drawn_inputs(seed))
    spreads = {}
    factors = {'g_mix': 3.067,
     'conv_ln_g': 6.317,
     'conv_ln_b': 4.026,
     'g_xattn': 8.0,
     'g_mem': 8.0,
     'g_final': 185.002,
     'g_ffn': 8.0,
     'b_router': 64.0}
    for name, (base, spread) in spreads.items():
        noise = np.random.default_rng([zlib.crc32(name.encode()), seed]).standard_normal(out[name].shape)
        drawn = base * np.exp(spread * noise) if base else spread * noise
        out[name] = jnp.asarray(drawn.astype(out[name].dtype))
    for name, factor in factors.items():
        out[name] = (out[name] * factor).astype(out[name].dtype)
    return out
```

```python
from contextlib import ExitStack

import concourse.bass as bass
from concourse import mybir


F32 = mybir.dt.float32
F32R = mybir.dt.float32r
I32 = mybir.dt.int32
ALU = mybir.AluOpType
ACT = mybir.ActivationFunctionType
X_AXIS = mybir.AxisListType.X

P = 128
EPS = 1e-6
UNIT = 2048
RING_A = 4
RING_M = 11
HL = 3


class BankPlan:

    def __init__(self):
        self.used = [0] * 8
        self.of = {}
        self.before = {}
        self.last = [None] * 8

    def add(self, label, bank):
        self.used[bank] += 1
        assert label not in self.of, label
        self.of[label] = (bank, self.used[bank])
        self.before[label], self.last[bank] = self.last[bank], label


def stream_plan(depth, n_blocks):
    units = []
    for L in range(depth):
        units += [("a", L, 0), ("b", L, 0), ("a", L, 1), ("b", L, 1), ("pin", L, 0), ("pin", L, 1)]
        units += [("gate", L, j) for j in range(8)]
        units += [("wpool", L, 0)]
        units += [("k", L, j) for j in range(4)]
        units += [("v", L, j) for j in range(2)]
        units += [("cout", L, j) for j in range(2)]
        units += [("mix", L, j) for j in range(4)]
        units += [("v", L, 2)]
        units += [("q", L, j) for j in range(4)]
        units += [("v", L, 3)]
        units += [("xo", L, j) for j in range(4)]
        if L % 2 == 0:
            units += ffn_units(L, n_blocks)
    return units


def ffn_units(L, n_blocks):
    units = []
    for b in range(n_blocks):
        units += [("gu", L, 2 * b), ("gu", L, 2 * b + 1)]
        if b:
            units += [("down", L, b - 1)]
    return units + [("down", L, n_blocks - 1)]


def trunk(nc, x, mem, g_mix, w_in, w_pool, pool_scale, w_dw, b_dw, conv_ln_g, conv_ln_b, w_conv_out,
          w_mix_out, g_xattn, g_mem, w_xq, w_xkv, w_xo, g_ffn, w_ffn_gu, w_ffn_down, w_router,
          b_router, w_moe_gu, w_moe_down, g_final, out):
    DEPTH, D = g_mix.shape
    S = x.shape[1]
    KC = D // P
    NT = S // P
    CW = w_dw.shape[3]
    CC = CW // P
    TAPS = w_dw.shape[1]
    PAD = TAPS - 1
    WINDOWS = (2, 4, 8, 16)
    PPAD = max(WINDOWS)
    NH = 4
    HD = D // NH
    FF = w_ffn_down.shape[1]
    FB = 256
    NB = FF // FB
    NE = w_moe_gu.shape[1]
    VROWS = 4 * DEPTH * KC + DEPTH * KC + 3 * DEPTH * CC
    assert (D, S, CW, DEPTH, NE) == (1024, 256, 512, 2, 8) and NB * FB == FF and VROWS <= P

    units = stream_plan(DEPTH, NB)
    NA = len(units)
    index = {u: n for n, u in enumerate(units)}
    moe = [(kind, i) for kind, _, i in ffn_units(1, NB)]
    NM = len(moe)
    assert NM % RING_M == 0 and NM % HL == 0

    plan = BankPlan()
    plan.add(("vec",), 0)
    rot = 0
    N_MIX, N_MEM, N_XATTN, N_FFN = 0, 1, 2, 3
    def norm_id(kind, L):
        return {"mix": (0, 4), "mem": (1, 1), "xattn": (2, 5), "ffn": (3, 6), "final": (7, 7)}[kind][L]
    def plan_norm(kind, L):
        for b in range(4):
            plan.add(("norm", norm_id(kind, L), b), 4 + b)
    plan_norm("mix", 0)
    for (kind, L, j) in units:
        if kind in ("a", "b"):
            plan.add((kind, L, j), 2 * j + (kind == "b"))
        elif kind == "pin":
            plan.add((kind, L, j), j)
        elif kind == "gate":
            plan.add((kind, L, j), (2 + j) % 4)
            if L == 0 and j == 1:
                plan_norm("mem", 0)
        elif kind == "wpool":
            for b in range(4):
                plan.add((kind, L, b), b)
        elif kind == "k":
            plan.add((kind, L, j), j)
            if j == 3:
                plan.add(("mean", L), 4)
        elif kind == "cout":
            for b in (2 * j, 2 * j + 1):
                plan.add((kind, L, b), b)
        elif kind in ("mix", "xo") and j % 2 == 0:
            for t in range(NT):
                plan.add((kind, L, j // 2, t), (4 if kind == "mix" else 0) + j + t)
        elif kind == "v" and j % 2 == 0:
            for t in range(NT):
                plan.add((kind, L, j // 2, t), (6, 2)[j // 2] + t)
        elif kind == "q":
            plan.add((kind, L, j), j % 2)
        elif kind == "gu" and j % 2 == 0:
            for t in range(NT):
                plan.add(("gu", L, j // 2, t), t)
        if (kind, j) == ("v", 0):
            plan.add(("var", L), 5)
        if (kind, j) == ("v", 2):
            plan_norm("xattn", L)
        if (kind, j) == ("q", 3):
            for b in range(4):
                plan.add(("score", L, b), 4 + b)
        if (kind, j) == ("v", 3):
            for b in range(4):
                plan.add(("pT", L, b), b)
            for b in range(4):
                plan.add(("pv", L, b), 4 + b)
        if (kind, j) == ("xo", 3):
            if L == 1:
                for n in range(2):
                    plan.add(("gb", n), n)
            plan_norm("ffn", L)
        if kind == "gu" and j % 2 == 1:
            plan.add(("hT", L, j // 2), 2)
            if j == 1:
                for t in range(NT):
                    for n in range(2):
                        plan.add(("ffn", L, n, t), 4 + 2 * n + t)
        if kind == "down" and j == NB - 1:
            plan_norm("mix", 1)
    plan.add(("logits",), 0)
    plan.add(("rank",), 1)
    plan.add(("count",), 2)
    for b in range(2):
        plan.add(("gather", b), 5 + b)
    base = list(plan.used)
    per = BankPlan()
    for b in range(NB):
        per.add(("gu", b), b % 2)
        if b == 1:
            per.add(("PT",), 7)
        if b:
            per.add(("hT", b - 1), 2)
        if b == 1:
            per.add(("y", 0), 3)
            per.add(("y", 1), 4)
    per.add(("hT", NB - 1), 2)
    per.add(("gather", 0), 5)
    per.add(("gather", 1), 6)
    SC_BANK = (7, 2, 5, 6)
    for r in range(4):
        per.add(("scatter", r), SC_BANK[r])

    raw_use, slot_uses = [], [0] * RING_M
    for n in range(NA):
        slot_uses[n % RING_A] += 1
        raw_use.append(slot_uses[n % RING_A])
    raw_base = list(slot_uses)
    PER_SLOT = NM // RING_M

    with ExitStack() as ctx:
        def sb(name, shape, dt=F32):
            return ctx.enter_context(nc.sbuf_tensor(name, shape, dt))

        def sem(name):
            return ctx.enter_context(nc.semaphore(name))

        bank = [ctx.enter_context(nc.psum_tensor(f"bank{b}", [P, 512], F32)) for b in range(8)]
        bank_full = [sem(f"bank_full{b}") for b in range(8)]

        arena = sb("arena", [P, RING_M * UNIT])
        raw = [arena[:, s * UNIT:(s + 1) * UNIT] for s in range(RING_M)]
        at = RING_A * UNIT
        def carve(n):
            nonlocal at
            at += n
            assert at <= RING_M * UNIT
            return arena[:, at - n:at]
        gate_b = carve(16 * S)
        gates = gate_b.rearrange("p (c s) -> p c s", s=S)
        qT = gates[:, 0:8, :]
        prob = gates[:, 8:16, :]
        kv_b = carve(16 * S)
        kT = kv_b[:, 0:8 * S].rearrange("p (c s) -> p c s", s=S)
        pT = kT
        v_sb = kv_b[:, 8 * S:16 * S].rearrange("p (t d) -> p t d", t=NT)
        mem_b = carve(8 * S)
        memT = mem_b.rearrange("p (c s) -> p c s", s=S)
        mem_in = mem_b.rearrange("p (t d) -> p t d", t=NT)
        cu_b = carve(CC * (PAD + S))
        cu = cu_b.rearrange("p (c s) -> p c s", c=CC)
        pu_b = carve(CC * (PPAD + S))
        pu = pu_b.rearrange("p (c s) -> p c s", c=CC)
        W1, W2 = CC * (PPAD + S), (CC - 1) * (PPAD + S)
        assert W1 + W2 <= 8 * S
        s1 = kv_b[:, 8 * S:8 * S + W1].rearrange("p (c s) -> p c s", c=CC)
        s2 = kv_b[:, 8 * S + W1:8 * S + W1 + W2].rearrange("p (c s) -> p c s", c=CC - 1)
        acc_b = carve(CC * S)
        acc = acc_b.rearrange("p (c s) -> p c s", c=CC)
        sqc = cu[:, :, PAD:PAD + S]
        sgc = pu[:, :, PPAD:PPAD + S]
        rows = gate_b[:, 0:3 * P].rearrange("p (r n) -> p r n", r=3)

        WH = sb("WH", [P, HL, UNIT], F32R)
        WL = sb("WL", [P, HL, UNIT], F32R)
        xs = sb("xs", [P, NT, D])
        xn = sb("xn", [P, NT, D])
        XH = sb("XH", [P, KC, S], F32R)
        XL = sb("XL", [P, KC, S], F32R)
        MH = sb("MH", [P, KC * S], F32R)
        ML = sb("ML", [P, KC * S], F32R)
        mTh = MH[:, :].rearrange("p (c s) -> p c s", s=S)
        mTl = ML[:, :].rearrange("p (c s) -> p c s", s=S)
        xnh = MH[:, :].rearrange("p (t d) -> p t d", t=NT)
        xnl = ML[:, :].rearrange("p (t d) -> p t d", t=NT)
        SH = sb("SH", [P, CC, S], F32R)
        SL = sb("SL", [P, CC, S], F32R)
        yh = SH[:, :, :].rearrange("p (n a) s -> p n (a s)", n=2)
        yl = SL[:, :, :].rearrange("p (n a) s -> p n (a s)", n=2)
        sh = sb("sh", [P, 4, FB])
        sg = sh[:, 0:2, :]
        hh = sh[:, 2:4, :]
        PM = sh[:, 3, :].rearrange("p (t s) -> p t s", t=NT)
        hTh = sb("hTh", [P, 2, S], F32R)
        hTl = sb("hTl", [P, 2, S], F32R)
        PMr = hTh[:, 1, :].rearrange("p (t s) -> p t s", t=NT)
        PT = hTl[:, 1, :]
        ident = sb("ident", [P, P])
        upper = sb("upper", [P, P])
        ones = sb("ones", [P, P])
        iota = sb("iota", [P, P])
        vec = sb("vec", [P, VROWS + DEPTH * TAPS * CC])
        icnt = sb("icnt", [P, CC, PPAD])
        m16 = sb("m16", [P, CC, PPAD])
        ss = sb("ss", [P, 8, NT, 2])
        mhalf = sb("mhalf", [P, NT])
        vv = sb("vv", [P, 8, NT])
        rs = sb("rs", [P, 8, NT])
        wr = sb("wr", [P, KC, NE])
        wrh = sb("wrh", [P, KC, NE], F32R)
        wrl = sb("wrl", [P, KC, NE], F32R)
        brow = sb("brow", [1, NE])
        lg = sb("lg", [P, 12, NT, NE])
        m12 = sb("m12", [P, 8, NT])
        slotT = sb("slotT", [P, NT, 2 * NE + 1])
        combT = sb("combT", [P, NT, 2 * NE])
        cur = sb("cur", [P, 2, NT])
        cnts = sb("cnts", [P, 4])
        n_it = sb("n_it", [1, 1], I32)
        smx = sb("smx", [P, 3, 8])

        GC = {"mix": 0, "xattn": DEPTH * KC, "mem": 2 * DEPTH * KC, "ffn": 3 * DEPTH * KC}
        PS0 = 4 * DEPTH * KC
        BD0 = PS0 + DEPTH * KC
        LG0 = BD0 + DEPTH * CC
        LB0 = LG0 + DEPTH * CC

        def gcol(kind, L, c):
            return vec[:, GC[kind] + L * KC + c:GC[kind] + L * KC + c + 1]

        def col(at0, L, width, c):
            return vec[:, at0 + L * width + c:at0 + L * width + c + 1]

        def tap(L, k, c):
            o = VROWS + (L * TAPS + k) * CC + c
            return vec[:, o:o + 1]

        raw_landed = [sem(f"raw_landed{s}") for s in range(RING_M)]
        hi_ready, lo_ready, unit_used = sem("hi_ready"), sem("lo_ready"), sem("unit_used")
        x_in = [sem(f"x_in{t}") for t in range(NT)]
        mem_in_s, rows_in, router_in, grow_in, gfin_in = (sem(n) for n in (
            "mem_landed", "rows_in", "router_in", "grow_in", "gfin_in"))
        c_id0, c_id, c_one, c_iota, c_cnt0, c_cnt, c_pad, vec_ready = (sem(n) for n in (
            "const_zeroed", "const_ident", "const_ones", "const_iota", "count_iota", "count_ready",
            "pads_zero", "vec_ready"))
        c_half = sem("const_minus_half")
        sq_done, var_ready, rstd_ready, xn_ready, ht_hi, ht_lo = (sem(n) for n in (
            "sq_done", "var_ready", "rstd_ready", "xn_ready", "ht_hi", "ht_lo"))
        mT_hi, mT_lo, sig_b, cu_ready, gate_ready, pu_ready = (sem(n) for n in (
            "mT_hi", "mT_lo", "sig_b", "cu_ready", "gate_ready", "pu_ready"))
        pool_step, pooled_hi, pooled_lo, zp_ready, conv_step = (sem(n) for n in (
            "pool_step", "pooled_hi", "pooled_lo", "zpool_ready", "conv_step"))
        cen_ready, csq_ready, cvar, cstd, crstd, cnorm, csilu, s_hi, s_lo = (sem(n) for n in (
            "conv_centred", "conv_squared", "conv_var", "conv_std", "conv_rstd", "conv_normed", "conv_silu",
            "s_hi", "s_lo"))
        zc_ready, z_ready, z_hi, z_lo, x_add, kT_ready, v_ready, qT_ready = (sem(n) for n in (
            "zc_ready", "z_ready", "z_hi", "z_lo", "x_add", "kT_ready", "v_ready", "qT_ready"))
        mx_ready, nmx_ready, p_exp, rden, p_norm, pT_ready, o_hi, o_lo = (sem(n) for n in (
            "mx_ready", "nmx_ready", "p_exp", "rden", "p_norm", "pT_ready", "o_hi", "o_lo"))
        silu_done, h_ready, hT_hi, hT_lo = (sem(n) for n in ("silu_done", "h_ready", "hT_hi", "hT_lo"))
        tab_ready, xnh_ready, xnl_ready, wr_hi, wr_lo, route, ex_ready, sel_ready = (sem(n) for n in (
            "table_ready", "xnh_ready", "xnl_ready", "wr_hi", "wr_lo", "route", "ex_ready", "sel_ready"))
        zero_ready = sem("zero_ready")
        nit_ready, cur_ready, PM_ready, PMr_ready, PT_ready, g_hi, g_lo, y_hi, y_lo, out_ready, stored = (
            sem(n) for n in ("nit_ready", "cur_ready", "PM_ready", "PMr_ready", "PT_ready", "gather_hi",
                             "gather_lo", "y_hi", "y_lo", "out_ready", "stored"))

        ROUTE_RANK, ROUTE_COUNT = 17, 22
        POOL_STEPS = 2 + 5 * CC

        def full(label):
            b, k = plan.of[label]
            return bank_full[b], k

        def mfull(label, it):
            b, k = per.of[label]
            return bank_full[b], it * per.used[b] + (base[b] + k)

        def bk(label):
            return bank[(plan.of.get(label) or per.of.get(label))[0]]

        def last_result(kind, L, j):
            if kind in ("a", "b", "pin", "gate", "k", "q"):
                return (kind, L, j)
            if kind == "wpool":
                return (kind, L, 3)
            if kind == "cout":
                return (kind, L, 2 * j + 1)
            if kind in ("mix", "xo", "v") and j % 2:
                return (kind, L, j // 2, NT - 1)
            if kind == "gu" and j % 2:
                return (kind, L, j // 2, NT - 1)
            if kind == "down" and j == NB - 1:
                return ("ffn", L, 1, NT - 1)
            return None

        n_used, used_at = 0, []
        for u in units:
            n_used += last_result(*u) is None
            used_at.append(n_used)
        used_base, n_used, moe_used = n_used, 0, []
        for (kind, j) in moe:
            n_used += (kind == "gu" and j % 2 == 0) or (kind == "down" and j < NB - 1)
            moe_used.append(n_used)
        used_per = n_used

        def through(n):
            label = last_result(*units[n])
            return full(label) if label else (unit_used, used_at[n])

        def mthrough(i, it):
            off, (kind, j) = i // NM, moe[i % NM]
            label = ("gu", j // 2) if kind == "gu" and j % 2 else ("y", 1) if (kind, j) == ("down", NB - 1) else None
            if label:
                b, k = per.of[label]
                return bank_full[b], it * per.used[b] + (off * per.used[b] + base[b] + k)
            return unit_used, it * used_per + (off * used_per + used_base + moe_used[i % NM])

        def xadd(L, stage, i):
            return 12 * L + {"mix": 0, "xo": 4, "ffn": 8}[stage] + i + 1

        def read(label):
            kind, *r = label
            if kind == "vec":
                return vec_ready, 1
            if kind == "norm":
                N, b = r
                return (ht_hi if N == norm_id("mem", 0) else ht_lo), 4 * N + b + 1
            if kind in ("gb", "logits", "rank", "count", "gather"):
                return {"gb": (xn_ready, 2 * norm_id("ffn", 1) + 2), "logits": (sel_ready, 3),
                        "rank": (route, ROUTE_RANK), "count": (route, ROUTE_COUNT),
                        "gather": (g_lo, r[0] + 1 if r else 0)}[kind]
            L = r[0]
            if kind in ("mix", "xo", "ffn"):
                return x_add, xadd(L, kind, 2 * r[1] + r[2] if kind != "ffn" else 2 * r[2] + r[1])
            return {
                "a": lambda j: (cu_ready, 2 * L + j + 1),
                "b": lambda j: (sig_b, 2 * L + j + 1),
                "pin": lambda j: (pu_ready, 2 * L + j + 1),
                "gate": lambda j: (gate_ready, 8 * L + j + 1),
                "wpool": lambda b: (zp_ready, 8 * L + 2 * b + 2),
                "k": lambda j: (kT_ready, 4 * L + j + 1),
                "mean": lambda: (cen_ready, L + 1),
                "var": lambda: (cvar, L + 1),
                "cout": lambda b: (zc_ready, 4 * L + b + 1),
                "v": lambda m, t: (v_ready, 4 * L + 2 * m + t + 1),
                "q": lambda j: (qT_ready, 4 * L + j + 1),
                "score": lambda b: (p_exp, 8 * L + 2 * b + 2),
                "pT": lambda h: (pT_ready, 4 * L + h + 1),
                "pv": lambda h: (o_lo, 4 * L + h + 1),
                "gu": lambda b, t: (h_ready, 2 * b + t + 1),
                "hT": lambda b: (hT_lo, b + 1),
            }[kind](*r[1:])

        def mread(label, back, it):
            kind, *r = label
            s, n, k = {
                "gu": lambda b: (h_ready, NB, 2 * NB + b + 1),
                "hT": lambda b: (hT_lo, NB, NB + b + 1),
                "PT": lambda: (PT_ready, 1, 1),
                "y": lambda m: (y_lo, 2, 2 + m + 1),
                "gather": lambda b: (g_lo, 2, 2 + b + 1),
                "scatter": lambda q: (x_add, 4, xadd(1, "ffn", q)),
            }[kind](*r)
            return s, it * n + (k - n * back)

        def wsrc(kind, L, j):
            if kind in ("a", "b", "pin", "gate"):
                c0 = {"pin": 0, "a": CW, "b": 2 * CW, "gate": 3 * CW}[kind] + j * 256
                return w_in[L].rearrange("(k p) n -> p k n", p=P)[:, :, c0:c0 + 256]
            if kind in ("k", "q"):
                w = w_xkv if kind == "k" else w_xq
                return w[L].rearrange("(k p) n -> p k n", p=P)[:, :, j * 256:j * 256 + 256]
            if kind == "wpool":
                return w_pool[L].rearrange("g p n -> p g n")
            if kind == "cout":
                return w_conv_out[L].rearrange("(k p) n -> p k n", p=P)[:, :, j * 512:j * 512 + 512]
            if kind in ("mix", "xo", "v"):
                w = {"mix": w_mix_out, "xo": w_xo, "v": w_xkv}[kind]
                c0 = (D if kind == "v" else 0) + (j // 2) * 512
                return w[L].rearrange("(k p) n -> p k n", p=P)[:, 4 * (j % 2):4 * (j % 2) + 4, c0:c0 + 512]
            if kind == "gu":
                return gu_src(w_ffn_gu[L // 2], j)
            return w_ffn_down[L // 2].rearrange("(b k p) n -> b p k n", k=2, p=P)[j]

        def gu_src(w, j):
            v = w.rearrange("(k p) (s f) -> p k s f", p=P, s=2)
            return v[:, 4 * (j % 2):4 * (j % 2) + 4, :, (j // 2) * FB:(j // 2) * FB + FB]

        def wdst(kind, slot):
            r = raw[slot]
            if kind in ("a", "b", "pin", "gate", "k", "q"):
                return r.rearrange("p (k n) -> p k n", k=8)
            if kind == "wpool":
                return r[:, 0:1024].rearrange("p (g n) -> p g n", g=4)
            if kind == "gu":
                return r.rearrange("p (k s f) -> p k s f", k=4, s=2)
            if kind == "down":
                return r.rearrange("p (k n) -> p k n", k=2)
            return r.rearrange("p (k n) -> p k n", k=4)

        def width(n):
            return 1024 if n < NA and units[n][0] == "wpool" else UNIT

        block = ctx.enter_context(nc.Block())

        @block.sync
        def _(sp):
            for t in range(NT):
                sp.dma_start(xs[:, t, :], x[0].rearrange("(t p) d -> p t d", p=P)[:, t]).then_inc(x_in[t], 16)
            for n, (kind, L, j) in enumerate(units):
                if n >= RING_A:
                    sp.wait_ge(lo_ready, n - RING_A + 1)
                dst, src = wdst(kind, n % RING_A), wsrc(kind, L, j)
                if kind == "gu":
                    for s in range(2):
                        sp.dma_start(dst[:, :, s, :], src[:, :, s, :]).then_inc(raw_landed[n % RING_A], 8 * 2)
                else:
                    sp.dma_start(dst, src).then_inc(raw_landed[n % RING_A], 16)

            def load_expert_unit(e, i):
                kind, j = moe[i]
                s = i % RING_M
                dst = wdst(kind, s)
                if kind == "gu":
                    w = w_moe_gu[0].rearrange("e (k p) (s f) -> e p k s f", p=P, s=2)
                    k0, f0 = 4 * (j % 2), (j // 2) * FB
                    for h in range(2):
                        src = w[bass.ds(e, 1), :, k0:k0 + 4, h, f0:f0 + FB].rearrange("o p k f -> (o p) k f")
                        sp.dma_start(dst[:, :, h, :], src).then_inc(raw_landed[s], 16)
                else:
                    w = w_moe_down[0].rearrange("e (b k p) n -> e b p k n", k=2, p=P)
                    src = w[bass.ds(e, 1), j].rearrange("o p k n -> (o p) k n")
                    sp.dma_start(dst, src).then_inc(raw_landed[s], 16)

            sp.wait_ge(s_lo, CC * DEPTH)
            sp.wait_ge(o_lo, 4 * DEPTH)
            for i in range(RING_A, RING_M):
                load_expert_unit(0, i)
            for i in range(RING_A):
                sp.wait_ge(lo_ready, max(n for n in range(NA) if n % RING_A == i) + 1)
                load_expert_unit(0, i)
            for i in range(RING_M, NM):
                sp.wait_ge(lo_ready, NA + i - RING_M + 1)
                load_expert_unit(0, i)
            sp.wait_ge(nit_ready, 1)
            n = sp.value_load(n_it[0:1, 0:1], min_val=NE, max_val=2 * NE)
            with sp.Fori(1, n) as it:
                for i in range(NM):
                    sp.wait_ge(lo_ready, it * NM + (NA + i - RING_M + 1))
                    load_expert_unit(it % NE, i)
            for i in range(2):
                sp.wait_ge(lo_ready, n * NM + (NA + i - RING_M + 1))
                load_expert_unit(0, i)
            for t in range(NT):
                sp.wait_ge(out_ready, t + 1)
                sp.dma_start(out[0].rearrange("(t p) d -> p t d", p=P)[:, t], xn[:, t]).then_inc(stored, 16)
            sp.wait_ge(stored, 16 * NT)

        LANDS = {"gu": 32}

        landed = [0] * RING_M
        dense_landed = []
        for n, (kind, L, j) in enumerate(units):
            landed[n % RING_A] += LANDS.get(kind, 16)
            dense_landed.append(landed[n % RING_A])
        landed_base = list(landed)
        moe_landed, per_slot = [], [0] * RING_M
        for i, (kind, j) in enumerate(moe):
            per_slot[i % RING_M] += LANDS.get(kind, 16)
            moe_landed.append(per_slot[i % RING_M])

        @block.gpsimd
        def _(pool):
            g = nc.gpsimd
            g.memset(ident[:, :], 0.0).then_inc(c_id0, 1)
            g.memset(upper[:, :], 1.0).then_inc(c_id0, 1)
            g.memset(ones[:, :], 1.0).then_inc(c_one, 1)
            pool.wait_ge(c_id0, 2)
            g.affine_select(out=ident[:, :], in_=ident[:, :], compare_op=ALU.not_equal, fill=1.0, base=0,
                            pattern=[[-1, P]], channel_multiplier=1).then_inc(c_id, 1)
            g.affine_select(out=upper[:, :], in_=upper[:, :], compare_op=ALU.is_gt, fill=0.0, base=0,
                            pattern=[[1, P]], channel_multiplier=-1).then_inc(c_id, 1)
            g.iota(iota[:, :], pattern=[[1, P]], base=0, channel_multiplier=0,
                   allow_small_or_imprecise_dtypes=True).then_inc(c_iota, 1)
            g.iota(m16[:, :, :], pattern=[[0, CC], [1, PPAD]], base=1, channel_multiplier=0,
                   allow_small_or_imprecise_dtypes=True).then_inc(c_cnt0, 1)
            g.memset(cu[:, :, 0:PAD], 0.0).then_inc(c_pad, 1)
            g.memset(pu[:, :, 0:PPAD], 0.0).then_inc(c_pad, 1)
            pool.wait_ge(c_cnt0, 1)
            for c, w in enumerate(WINDOWS):
                g.tensor_scalar(m16[:, c, :], m16[:, c, :], float(w), None, ALU.min).then_inc(c_cnt0, 1)
            g.memset(mhalf[:, :], -0.5).then_inc(c_half, 1)
            pool.wait_ge(c_half, 1)

            def rstd(N):
                pool.wait_ge(var_ready, N + 1)
                g.tensor_tensor(rs[:, N, :], vv[:, N, :], mhalf[:, :], ALU.pow).then_inc(rstd_ready, 1)

            rstd(0)
            for L in range(DEPTH):
                o = L * POOL_STEPS
                pool.wait_ge(pu_ready, 2 * L + 2)
                if L:
                    pool.wait_ge(o_lo, 4 * L)
                g.memset(s1[:, :, 0:PPAD], 0.0).then_inc(pool_step, 1)
                g.memset(s2[:, :, 0:PPAD], 0.0).then_inc(pool_step, 1)
                views = ((pu, 0), (s1, 0), (s2, 1), (s1, 0), (s2, 1))
                for i in range(CC):
                    lag = 1 << i
                    (src, s0), (dst, d0) = views[i], views[i + 1]
                    pool.wait_ge(pool_step, o + 2 + i)
                    g.tensor_tensor(dst[:, i - d0:CC - d0, PPAD:PPAD + S], src[:, i - s0:CC - s0, PPAD:PPAD + S],
                                    src[:, i - s0:CC - s0, PPAD - lag:PPAD + S - lag],
                                    ALU.add).then_inc(pool_step, 1)
                pool.wait_ge(pool_step, o + 2 + CC)
                pool.wait_ge(c_cnt, 1)
                for c in range(CC):
                    w, w0 = views[c + 1]
                    g.tensor_tensor(m16[:, c, :], w[:, c - w0, PPAD:2 * PPAD], icnt[:, c, :],
                                    ALU.mult).then_inc(pool_step, 1)
                    g.tensor_scalar(w[:, c - w0, 2 * PPAD:], w[:, c - w0, 2 * PPAD:], 1.0 / WINDOWS[c], None,
                                    ALU.mult).then_inc(pool_step, 1)
                pool.wait_ge(pool_step, o + 2 + 3 * CC)
                for c in range(CC):
                    w, w0 = views[c + 1]
                    g.tensor_tensor(w[:, c - w0, PPAD:2 * PPAD], m16[:, c, :], pu[:, c, PPAD:2 * PPAD],
                                    ALU.subtract).then_inc(pool_step, 1)
                    g.tensor_tensor(w[:, c - w0, 2 * PPAD:], w[:, c - w0, 2 * PPAD:], pu[:, c, 2 * PPAD:],
                                    ALU.subtract).then_inc(pool_step, 1)
                if L == 0:
                    rstd(norm_id("mem", 0))
                rstd(norm_id("xattn", L))
                rstd(norm_id("ffn", L))
                if L == 0:
                    rstd(norm_id("mix", 1))
            rstd(norm_id("final", 0))

        @block.scalar
        def _(act):
            a = nc.scalar
            r = 0
            for src in (g_mix, g_xattn, g_mem, g_ffn, pool_scale, b_dw, conv_ln_g, conv_ln_b):
                v = src.rearrange("l (k p) -> (l k) p", p=P)
                act.dma_start(rows[r:r + v.shape[0], 0, :], v).then_inc(rows_in, 16)
                r += v.shape[0]
            for L in range(DEPTH):
                act.dma_start(rows[0:TAPS * CC, 1 + L, :],
                              w_dw[L].rearrange("k o (c p) -> (k o c) p", p=P)).then_inc(rows_in, 16)
            act.dma_start(wr[:, :, :], w_router[0].rearrange("(k p) e -> p k e", p=P)).then_inc(router_in, 16)
            act.dma_start(brow[:, :], b_router).then_inc(router_in, 16)

            def hi(n):
                if n >= NA:
                    i = n - NA
                    act.wait_ge(raw_landed[i % RING_M], landed_base[i % RING_M] + moe_landed[i])
                else:
                    act.wait_ge(raw_landed[n % RING_A], dense_landed[n])
                if n >= HL:
                    act.wait_ge(*through(n - HL))
                s = raw[n % RING_A] if n < NA else raw[(n - NA) % RING_M]
                a.activation(WH[:, n % HL, 0:width(n)], s[:, 0:width(n)], ACT.Copy).then_inc(hi_ready, 1)

            def squares(N, src, pieces, ready):
                for i, (m, t) in enumerate(pieces):
                    act.wait_ge(*ready(i, t))
                    ms = slice(m * 512, m * 512 + 512)
                    a.activation(xn[:, t, ms], src[:, t, ms], ACT.Square, scale=D ** -0.5,
                                 accum_out=ss[:, N, t, m:m + 1]).then_inc(sq_done, 1)

            BY_HALF = [(m, t) for m in range(2) for t in range(NT)]
            BY_TILE = [(m, t) for t in range(NT) for m in range(2)]

            def norm_hi(kind, L, out, scaled=True):
                N = norm_id(kind, L)
                for b in range(4):
                    act.wait_ge(*full(("norm", N, b)))
                    ps = bk(("norm", N, b))[:, :].rearrange("p (c s) -> p c s", c=2)
                    if not scaled:
                        ins = a.activation(out[:, 2 * b:2 * b + 2, :], ps, ACT.Copy)
                    else:
                        for c in range(2):
                            ins = a.activation(out[:, 2 * b + c, :], ps[:, c, :], ACT.Copy,
                                               scale=gcol(kind, L, 2 * b + c))
                    ins.then_inc(ht_hi, 1)

            def copy_hi(out, in_, full_label, s):
                act.wait_ge(*full(full_label))
                a.activation(out, in_, ACT.Copy).then_inc(s, 1)

            hi(0)
            hi(1)
            squares(norm_id("mix", 0), xs, BY_TILE, lambda i, t: (x_in[t], 16))
            act.dma_start(mem_in, mem[0].rearrange("(t p) d -> p t d", p=P)).then_inc(mem_in_s, 16)
            act.wait_ge(vec_ready, 1)
            norm_hi("mix", 0, XH)
            for n, (kind, L, j) in enumerate(units):
                hi(n + 2)
                if kind == "b":
                    act.wait_ge(*full(("b", L, j)))
                    a.activation(sg, bk(("b", L, j))[:, :].rearrange("p (c s) -> p c s", c=2),
                                 ACT.Sigmoid).then_inc(sig_b, 1)
                if kind == "a":
                    if L or j:
                        act.wait_ge(cu_ready, 2 * L + j)
                if kind == "pin":
                    act.wait_ge(*full(("pin", L, j)))
                    if L:
                        act.wait_ge(s_lo, CC * L)
                    a.activation(pu[:, 2 * j:2 * j + 2, PPAD:PPAD + S],
                                 bk(("pin", L, j))[:, :].rearrange("p (c s) -> p c s", c=2),
                                 ACT.Copy).then_inc(pu_ready, 1)
                if kind == "gate":
                    act.wait_ge(*full(("gate", L, j)))
                    a.activation(gates[:, 2 * j:2 * j + 2, :],
                                 bk(("gate", L, j))[:, :].rearrange("p (c s) -> p c s", c=2),
                                 ACT.Sigmoid).then_inc(gate_ready, 1)
                    if L == 0 and j == 0:
                        squares(norm_id("mem", 0), mem_in, BY_TILE, lambda i, t: (mem_in_s, 16))
                    if L == 0 and j == 2:
                        for b in range(4):
                            copy_hi(memT[:, 2 * b:2 * b + 2, :],
                                    bk(("norm", 1, b))[:, :].rearrange("p (c s) -> p c s", c=2),
                                    ("norm", 1, b), ht_hi)
                if (kind, L, j) in (("gate", 0, 4), ("gu", 0, 5)):
                    ML = 0 if kind == "gate" else 1
                    act.wait_ge(ht_hi, 4 * norm_id("mem", 0) + 4)
                    for c in range(KC):
                        a.activation(mTh[:, c, :], memT[:, c, :], ACT.Copy,
                                     scale=gcol("mem", ML, c)).then_inc(mT_hi, 1)
                if kind == "gate" and j == 5:
                    act.wait_ge(pool_step, POOL_STEPS * (L + 1))
                    a.activation(SH[:, 0:4:2, :], s1[:, 0:4:2, PPAD:PPAD + S], ACT.Copy).then_inc(pooled_hi, 1)
                    a.activation(SH[:, 1:4:2, :], s2[:, 0:3:2, PPAD:PPAD + S], ACT.Copy).then_inc(pooled_hi, 1)
                if kind == "k":
                    act.wait_ge(*full(("k", L, j)))
                    a.activation(kT[:, 2 * j:2 * j + 2, :],
                                 bk(("k", L, j))[:, :].rearrange("p (c s) -> p c s", c=2),
                                 ACT.Copy).then_inc(kT_ready, 1)
                    if j == 3:
                        act.wait_ge(cen_ready, L + 1)
                        a.activation(sqc, acc, ACT.Square).then_inc(csq_ready, 1)
                if (kind, j) == ("v", 0):
                    act.wait_ge(cvar, L + 1)
                    a.activation(sqc[:, 0, :], sqc[:, 1, :], ACT.Sqrt).then_inc(cstd, 1)
                    for c in range(CC):
                        act.wait_ge(cnorm, CC * L + c + 1)
                        a.activation(sgc[:, c, :], acc[:, c, :], ACT.Silu, bias=col(LB0, L, CC, c),
                                     scale=col(LG0, L, CC, c)).then_inc(csilu, 1)
                        if c:
                            act.wait_ge(csilu, CC * L + c)
                            a.activation(SH[:, c - 1, :], sgc[:, c - 1, :], ACT.Copy).then_inc(s_hi, 1)
                    act.wait_ge(csilu, CC * L + CC)
                    a.activation(SH[:, CC - 1, :], sgc[:, CC - 1, :], ACT.Copy).then_inc(s_hi, 1)
                if kind == "cout":
                    for b in (2 * j, 2 * j + 1):
                        act.wait_ge(z_ready, 4 * L + b + 1)
                        a.activation(XH[:, 2 * b:2 * b + 2, :], gates[:, 8 + 2 * b:10 + 2 * b, :],
                                     ACT.Copy).then_inc(z_hi, 1)
                if kind == "mix" and j % 2:
                    m = j // 2
                    squares(norm_id("xattn", L), xs, BY_HALF[2 * m:2 * m + 2],
                            lambda i, t: (x_add, xadd(L, "mix", 2 * m + i)))
                if kind == "xo" and j % 2:
                    m = j // 2
                    squares(norm_id("ffn", L), xs, BY_HALF[2 * m:2 * m + 2],
                            lambda i, t: (x_add, xadd(L, "xo", 2 * m + i)))
                if (kind, j) == ("v", 2):
                    norm_hi("xattn", L, XH)
                if kind == "q":
                    act.wait_ge(*full(("q", L, j)))
                    a.activation(qT[:, 2 * j:2 * j + 2, :],
                                 bk(("q", L, j))[:, :].rearrange("p (c s) -> p c s", c=2),
                                 ACT.Copy).then_inc(qT_ready, 1)
                if (kind, j) == ("q", 3):
                    for b in range(4):
                        act.wait_ge(nmx_ready, 4 * L + b + 1)
                        for h in range(2):
                            i = 2 * b + h
                            a.activation(prob[:, i, :], bk(("score", L, b))[:, h * S:h * S + S], ACT.Exp,
                                         bias=smx[:, 1, i:i + 1], scale=HD ** -0.5,
                                         accum_out=smx[:, 2, i:i + 1]).then_inc(p_exp, 1)
                if (kind, L, j) == ("xo", 1, 0):
                    act.dma_start(sh[0:1, :, :].rearrange("p a b -> p (a b)"), g_ffn[1:2, :]).then_inc(grow_in, 16)
                    act.wait_ge(router_in, 32)
                    a.activation(wrh[:, :, :], wr[:, :, :], ACT.Copy).then_inc(wr_hi, 1)
                if kind == "v" and j % 2 == 1:
                    for t in range(NT):
                        act.wait_ge(*full(("v", L, j // 2, t)))
                        a.activation(v_sb[:, t, (j // 2) * 512:(j // 2) * 512 + 512],
                                     bk(("v", L, j // 2, t))[:, :], ACT.Copy).then_inc(v_ready, 1)
                if (kind, j) == ("v", 3):
                    for h in range(NH):
                        act.wait_ge(*full(("pT", L, h)))
                        a.activation(pT[:, 2 * h:2 * h + 2, :],
                                     bk(("pT", L, h))[:, :].rearrange("p (c s) -> p c s", c=2),
                                     ACT.Copy).then_inc(pT_ready, 1)
                    for h in range(NH):
                        act.wait_ge(*full(("pv", L, h)))
                        a.activation(XH[:, 2 * h:2 * h + 2, :],
                                     bk(("pv", L, h))[:, :].rearrange("p (c s) -> p c s", c=2),
                                     ACT.Copy).then_inc(o_hi, 1)
                if (kind, j) == ("xo", 3):
                    if L == 1:
                        for t in range(NT):
                            act.wait_ge(xn_ready, 2 * norm_id("ffn", 1) + t + 1)
                            a.activation(xnh[:, t], xn[:, t], ACT.Copy).then_inc(xnh_ready, 1)
                    norm_hi("ffn", L, XH, scaled=(L == 0))
                if kind == "gu" and j % 2 == 1:
                    for t in range(NT):
                        act.wait_ge(*full(("gu", L, j // 2, t)))
                        if j > 1:
                            act.wait_ge(h_ready, 2 * (j // 2))
                        a.activation(sg[:, t, :], bk(("gu", L, j // 2, t))[:, 0:FB],
                                     ACT.Silu).then_inc(silu_done, 1)
                    if j == 1:
                        act.wait_ge(*full(("hT", L, 0)))
                        a.activation(hTh[:, :, :], bk(("hT", L, 0))[:, :].rearrange("p (c s) -> p c s", c=2),
                                     ACT.Copy).then_inc(hT_hi, 1)
                if kind == "down" and j < NB - 1:
                    act.wait_ge(*full(("hT", L, j + 1)))
                    a.activation(hTh[:, :, :], bk(("hT", L, j + 1))[:, :].rearrange("p (c s) -> p c s", c=2),
                                 ACT.Copy).then_inc(hT_hi, 1)
                if kind == "down" and j == NB - 1:
                    squares(norm_id("mix", 1), xs, BY_TILE,
                            lambda i, t: (x_add, xadd(0, "ffn", 2 * t + i % 2)))
                    norm_hi("mix", 1, XH)

            act.wait_ge(route, 7)
            a.activation(m12[:, 3, :], m12[:, 2, :], ACT.Exp).then_inc(ex_ready, 1)
            act.wait_ge(PM_ready, 1)
            a.activation(PMr, PM, ACT.Copy).then_inc(PMr_ready, 1)

            def gather_hi(banks, at_full):
                for b in banks:
                    act.wait_ge(*at_full(b))
                    a.activation(XH[:, 4 * b:4 * b + 4, 0:P],
                                 bank[5 + b][:, :].rearrange("p (c s) -> p c s", c=4), ACT.Copy).then_inc(g_hi, 1)
            gather_hi((0, 1), lambda b: full(("gather", b)))
            act.wait_ge(zero_ready, 1)
            a.activation(cnts[:, 3:4], cnts[:, 2:3], ACT.Silu).then_inc(tab_ready, 1)
            act.wait_ge(nit_ready, 1)
            n = act.value_load(n_it[0:1, 0:1], min_val=NE, max_val=2 * NE)
            with act.Fori(0, n) as it:
                act.wait_ge(tab_ready, it + 1)
                a.activation(cnts[:, 3:4], cnts[:, 2:3], ACT.Silu).then_inc(tab_ready, 1)

                def hi_m(i):
                    s = (i % NM) % RING_M
                    extra = per_slot[s] if i >= NM else 0
                    act.wait_ge(raw_landed[s], it * per_slot[s] + (landed_base[s] + extra + moe_landed[i % NM]))
                    act.wait_ge(*mthrough(i - HL, it))
                    a.activation(WH[:, (NA + i) % HL, :], raw[s], ACT.Copy).then_inc(hi_ready, 1)

                def hT_hi_m(b):
                    act.wait_ge(*mfull(("hT", b), it))
                    a.activation(hTh[:, 0, :], bank[2][:, 0:2 * P], ACT.Copy).then_inc(hT_hi, 1)

                for i, (kind, j) in enumerate(moe):
                    hi_m(i + 2)
                    b = j // 2
                    if kind == "gu" and j % 2 == 0 and b >= 1:
                        hT_hi_m(b - 1)
                    if kind == "gu" and j == 3:
                        act.wait_ge(*mfull(("PT",), it))
                        a.activation(PT, bank[7][:, 0:S], ACT.Copy).then_inc(PT_ready, 1)
                    if kind == "gu" and j % 2 == 1:
                        act.wait_ge(*mfull(("gu", b), it))
                        act.wait_ge(h_ready, it * NB + (2 * NB + b))
                        a.activation(sg[:, 0, :], bank[b % 2][:, 0:FB], ACT.Silu).then_inc(silu_done, 1)
                    if kind == "gu" and j == 2 * 8 + 1:
                        act.wait_ge(PM_ready, it + 2)
                        a.activation(PMr, PM, ACT.Copy).then_inc(PMr_ready, 1)
                    if kind == "down" and j == NB - 2:
                        hT_hi_m(NB - 1)
                        gather_hi((0,), lambda b: mfull(("gather", b), it))
                    if kind == "down" and j == NB - 1:
                        for m in range(2):
                            act.wait_ge(*mfull(("y", m), it))
                            a.activation(yh[:, m, :], bank[3 + m][:, :], ACT.Copy).then_inc(y_hi, 1)
                        gather_hi((1,), lambda b: mfull(("gather", b), it))

            act.wait_ge(h_ready, n * NB + 2 * NB)
            act.wait_ge(PM_ready, n + 1)
            act.dma_start(sh[0:1, :, :].rearrange("p a b -> p (a b)"),
                          g_final.rearrange("(o d) -> o d", o=1)).then_inc(gfin_in, 16)
            squares(norm_id("final", 0), xs, BY_HALF, lambda i, t: (x_add, n * 4 + xadd(1, "ffn", i - 4)))

        @block.vector
        def _(dve):
            v = nc.vector
            dve.wait_ge(c_cnt0, 1 + CC)
            v.reciprocal(icnt[:, :, :], m16[:, :, :]).then_inc(c_cnt, 1)
            dve.wait_ge(*full(("vec",)))
            v.tensor_copy(vec[:, 0:VROWS], bank[0][:, 0:VROWS]).then_inc(c_cnt, 1)
            v.tensor_copy(vec[:, VROWS:], bank[0][:, P:P + DEPTH * TAPS * CC]).then_inc(vec_ready, 1)
            dve.wait_ge(vec_ready, 1)

            def lo(n):
                dve.wait_ge(hi_ready, n + 1)
                s = raw[n % RING_A] if n < NA else raw[(n - NA) % RING_M]
                w = width(n)
                v.tensor_tensor(WL[:, n % HL, 0:w], s[:, 0:w], WH[:, n % HL, 0:w].bitcast(F32),
                                ALU.subtract).then_inc(lo_ready, 1)

            def norm_var(N):
                dve.wait_ge(sq_done, 4 * N + 4)
                v.scalar_tensor_tensor(vv[:, N, :], ss[:, N, :, 0], EPS, ss[:, N, :, 1], ALU.add,
                                       ALU.add).then_inc(var_ready, 1)
                dve.wait_ge(rstd_ready, N + 1)

            def norm_scale(N, src):
                norm_var(N)
                for t in range(NT):
                    v.tensor_scalar(xn[:, t], src[:, t], rs[:, N, t:t + 1], None, ALU.mult).then_inc(xn_ready, 1)

            def norm_lo(kind, L, out, hi, scaled=True):
                N = norm_id(kind, L)
                for b in range(4):
                    dve.wait_ge(ht_hi, 4 * N + b + 1)
                    ps = bk(("norm", N, b))[:, :].rearrange("p (c s) -> p c s", c=2)
                    if scaled:
                        for c in range(2):
                            k = 2 * b + c
                            ins = v.scalar_tensor_tensor(out[:, k, :], ps[:, c, :], gcol(kind, L, k),
                                                         hi[:, k, :].bitcast(F32), ALU.mult, ALU.subtract)
                    else:
                        ins = v.tensor_tensor(out[:, 2 * b:2 * b + 2, :], ps,
                                              hi[:, 2 * b:2 * b + 2, :].bitcast(F32), ALU.subtract)
                    ins.then_inc(ht_lo, 1)

            conv_n = [0]

            def conv_taps(L, count):
                for _ in range(count):
                    i = conv_n[0] - L * TAPS * CC
                    if i >= TAPS * CC:
                        return
                    k, c = divmod(i, CC)
                    if k == 0:
                        if c == 0:
                            dve.wait_ge(cu_ready, 2 * L + 2)
                        v.tensor_scalar(acc[:, c, :], cu[:, c, 0:S], tap(L, 0, c), col(BD0, L, CC, c),
                                        ALU.mult, ALU.add).then_inc(conv_step, 1)
                    else:
                        dve.wait_ge(conv_step, conv_n[0] - CC + 1)
                        v.scalar_tensor_tensor(acc[:, c, :], cu[:, c, k:k + S], tap(L, k, c), acc[:, c, :],
                                               ALU.mult, ALU.add).then_inc(conv_step, 1)
                    conv_n[0] += 1

            def add_x(L, stage, kind, halves):
                for m in halves:
                    for t in range(NT):
                        label = (kind, L, m, t)
                        dve.wait_ge(*full(label))
                        v.tensor_tensor(xs[:, t, m * 512:m * 512 + 512], xs[:, t, m * 512:m * 512 + 512],
                                        bk(label)[:, :], ALU.add).then_inc(x_add, 1)

            lo(0)
            lo(1)
            norm_scale(norm_id("mix", 0), xs)
            norm_lo("mix", 0, XL, XH)
            for n, (kind, L, j) in enumerate(units):
                if n + 2 < NA:
                    lo(n + 2)
                else:
                    lo(n + 2)
                if kind == "b":
                    dve.wait_ge(sig_b, 2 * L + j + 1)
                    dve.wait_ge(*full(("a", L, j)))
                    dve.wait_ge(c_pad, 2)
                    v.tensor_tensor(cu[:, 2 * j:2 * j + 2, PAD:PAD + S],
                                    bk(("a", L, j))[:, :].rearrange("p (c s) -> p c s", c=2), sg,
                                    ALU.mult).then_inc(cu_ready, 1)
                if kind == "pin":
                    conv_taps(L, 11)
                if kind == "gate":
                    if L == 0 and j == 0:
                        norm_scale(norm_id("mem", 0), mem_in)
                        dve.sem_inc(ht_lo, 4)
                    conv_taps(L, 9)
                if (kind, L, j) in (("gate", 0, 4), ("gu", 0, 5)):
                    ML = 0 if kind == "gate" else 1
                    for c in range(KC):
                        dve.wait_ge(mT_hi, 8 * ML + c + 1)
                        v.scalar_tensor_tensor(mTl[:, c, :], memT[:, c, :], gcol("mem", ML, c),
                                               mTh[:, c, :].bitcast(F32), ALU.mult,
                                               ALU.subtract).then_inc(mT_lo, 1)
                if kind == "gate" and j == 5:
                    dve.wait_ge(pooled_hi, 2 * L + 1)
                    v.tensor_tensor(SL[:, 0:4:2, :], s1[:, 0:4:2, PPAD:PPAD + S],
                                    SH[:, 0:4:2, :].bitcast(F32), ALU.subtract).then_inc(pooled_lo, 1)
                    dve.wait_ge(pooled_hi, 2 * L + 2)
                    v.tensor_tensor(SL[:, 1:4:2, :], s2[:, 0:3:2, PPAD:PPAD + S],
                                    SH[:, 1:4:2, :].bitcast(F32), ALU.subtract).then_inc(pooled_lo, 1)
                if kind == "wpool":
                    for b in range(4):
                        dve.wait_ge(*full(("wpool", L, b)))
                        for c in range(2):
                            k = 2 * b + c
                            v.scalar_tensor_tensor(gates[:, k, :], bk(("wpool", L, b))[:, c * S:c * S + S],
                                                   col(PS0, L, KC, k), gates[:, k, :], ALU.mult,
                                                   ALU.mult).then_inc(zp_ready, 1)
                    conv_taps(L, 4)
                if kind == "k":
                    conv_taps(L, TAPS * CC if j == 2 else 9)
                    if j == 3:
                        dve.wait_ge(*full(("mean", L)))
                        v.scalar_tensor_tensor(acc, bank[4][:, 0:S].unsqueeze(1).to_broadcast([P, CC, S]),
                                               -1.0 / CW, acc, ALU.mult, ALU.add).then_inc(cen_ready, 1)
                if (kind, j) == ("v", 0):
                    dve.wait_ge(*full(("var", L)))
                    v.tensor_scalar(sqc[:, 1, :], bank[5][:, 0:S], 1.0 / CW, EPS, ALU.mult, ALU.add).then_inc(cvar, 1)
                    dve.wait_ge(cstd, L + 1)
                    v.reciprocal(sqc[:, 2, :], sqc[:, 0, :]).then_inc(crstd, 1)
                    dve.wait_ge(crstd, L + 1)
                    for c in range(CC):
                        v.tensor_tensor(acc[:, c, :], acc[:, c, :], sqc[:, 2, :], ALU.mult).then_inc(cnorm, 1)
                    for c in range(CC):
                        dve.wait_ge(s_hi, CC * L + c + 1)
                        v.tensor_tensor(SL[:, c, :], sgc[:, c, :], SH[:, c, :].bitcast(F32),
                                        ALU.subtract).then_inc(s_lo, 1)
                if kind == "cout":
                    for b in (2 * j, 2 * j + 1):
                        label = ("cout", L, b)
                        dve.wait_ge(*full(label))
                        gc = gates[:, 8 + 2 * b:10 + 2 * b, :]
                        v.tensor_tensor(gc, bk(label)[:, :].rearrange("p (c s) -> p c s", c=2), gc,
                                        ALU.mult).then_inc(zc_ready, 1)
                        dve.wait_ge(zc_ready, 4 * L + b + 1)
                        v.tensor_tensor(gc, gc, gates[:, 2 * b:2 * b + 2, :], ALU.add).then_inc(z_ready, 1)
                        dve.wait_ge(z_hi, 4 * L + b + 1)
                        v.tensor_tensor(XL[:, 2 * b:2 * b + 2, :], gc, XH[:, 2 * b:2 * b + 2, :].bitcast(F32),
                                        ALU.subtract).then_inc(z_lo, 1)
                if kind == "mix" and j % 2:
                    add_x(L, "mix", "mix", (j // 2,))
                if (kind, j) == ("mix", 3):
                    norm_scale(norm_id("xattn", L), xs)
                if (kind, j) == ("v", 2):
                    norm_lo("xattn", L, XL, XH)
                if (kind, j) == ("q", 3):
                    for b in range(4):
                        dve.wait_ge(*full(("score", L, b)))
                        if L:
                            dve.wait_ge(p_norm, 8 * L)
                        v.tensor_reduce(smx[:, 0, 2 * b:2 * b + 2],
                                        bk(("score", L, b))[:, :].rearrange("p (c s) -> p c s", c=2),
                                        X_AXIS, ALU.max).then_inc(mx_ready, 1)
                        dve.wait_ge(mx_ready, 4 * L + b + 1)
                        v.tensor_scalar(smx[:, 1, 2 * b:2 * b + 2], smx[:, 0, 2 * b:2 * b + 2], -(HD ** -0.5), None,
                                        ALU.mult).then_inc(nmx_ready, 1)
                    for b in range(4):
                        dve.wait_ge(p_exp, 8 * L + 2 * b + 2)
                        v.reciprocal(smx[:, 2, 2 * b:2 * b + 2], smx[:, 2, 2 * b:2 * b + 2]).then_inc(rden, 1)
                        dve.wait_ge(rden, 4 * L + b + 1)
                        for i in (2 * b, 2 * b + 1):
                            v.tensor_scalar(prob[:, i, :], prob[:, i, :], smx[:, 2, i:i + 1], None,
                                            ALU.mult).then_inc(p_norm, 1)
                if (kind, j) == ("v", 3):
                    for h in range(NH):
                        dve.wait_ge(o_hi, 4 * L + h + 1)
                        v.tensor_tensor(XL[:, 2 * h:2 * h + 2, :],
                                        bk(("pv", L, h))[:, :].rearrange("p (c s) -> p c s", c=2),
                                        XH[:, 2 * h:2 * h + 2, :].bitcast(F32), ALU.subtract).then_inc(o_lo, 1)
                if kind == "xo" and j % 2:
                    add_x(L, "xo", "xo", (j // 2,))
                if (kind, j) == ("xo", 3):
                    if L == 0:
                        norm_scale(norm_id("ffn", 0), xs)
                        norm_lo("ffn", 0, XL, XH)
                    else:
                        dve.wait_ge(wr_hi, 1)
                        v.tensor_tensor(wrl[:, :, :], wr[:, :, :], wrh[:, :, :].bitcast(F32),
                                        ALU.subtract).then_inc(wr_lo, 1)
                        N = norm_id("ffn", 1)
                        norm_var(N)
                        for m in range(2):
                            dve.wait_ge(*full(("gb", m)))
                        for t in range(NT):
                            for m in range(2):
                                ins = v.scalar_tensor_tensor(xn[:, t, m * 512:m * 512 + 512],
                                                             xs[:, t, m * 512:m * 512 + 512], rs[:, N, t:t + 1],
                                                             bank[m][:, :], ALU.mult, ALU.mult)
                            ins.then_inc(xn_ready, 1)
                        for t in range(NT):
                            dve.wait_ge(xnh_ready, t + 1)
                            v.tensor_tensor(xnl[:, t], xn[:, t], xnh[:, t].bitcast(F32),
                                            ALU.subtract).then_inc(xnl_ready, 1)
                        norm_lo("ffn", 1, XL, XH, scaled=False)
                if kind == "gu" and j % 2 == 1:
                    b = j // 2
                    for t in range(NT):
                        dve.wait_ge(silu_done, 2 * b + t + 1)
                        if b:
                            dve.wait_ge(hT_hi, b)
                        v.tensor_tensor(hh[:, t, :], sg[:, t, :], bank[t][:, FB:2 * FB],
                                        ALU.mult).then_inc(h_ready, 1)
                    if j == 1:
                        dve.wait_ge(hT_hi, 1)
                        v.tensor_tensor(hTl[:, :, :], bank[2][:, :].rearrange("p (c s) -> p c s", c=2),
                                        hTh[:, :, :].bitcast(F32), ALU.subtract).then_inc(hT_lo, 1)
                if kind == "down" and j < NB - 1:
                    dve.wait_ge(hT_hi, j + 2)
                    v.tensor_tensor(hTl[:, :, :], bank[2][:, :].rearrange("p (c s) -> p c s", c=2),
                                    hTh[:, :, :].bitcast(F32), ALU.subtract).then_inc(hT_lo, 1)
                if kind == "down" and j == NB - 1:
                    for t in range(NT):
                        for m in range(2):
                            label = ("ffn", L, m, t)
                            dve.wait_ge(*full(label))
                            xv = xs[:, t, m * 512:m * 512 + 512]
                            v.tensor_tensor(xv, xv, bk(label)[:, :], ALU.add).then_inc(x_add, 1)
                    norm_scale(norm_id("mix", 1), xs)
                    norm_lo("mix", 1, XL, XH)

            rt = [0]

            def link(ins):
                rt[0] += 1
                ins.then_inc(route, 1)
                dve.wait_ge(route, rt[0])

            def wide(c):
                return m12[:, c, :].unsqueeze(2).to_broadcast([P, NT, NE])

            LOG, EQ, SC, F1, L2, F2, SEL, COM, RNK, TMP, PRI = (lg[:, i] for i in range(11))
            dve.wait_ge(c_iota, 1)
            dve.wait_ge(*full(("logits",)))
            logits = bank[0][:, 0:NT * NE].rearrange("p (t e) -> p t e", t=NT)

            def first_max(src, m, first):
                link(v.tensor_reduce(m12[:, m, :], src, X_AXIS, ALU.max))
                link(v.tensor_tensor(EQ, src, wide(m), ALU.is_equal))
                link(v.tensor_tensor(SC, EQ, PRI, ALU.mult))
                link(v.tensor_reduce(m12[:, 4, :], SC, X_AXIS, ALU.max))
                link(v.tensor_tensor(first, SC, wide(4), ALU.is_equal))

            for t in range(NT):
                v.tensor_scalar(PRI[:, t, :], iota[:, 0:NE], -1.0, float(NE), ALU.mult,
                                ALU.add).then_inc(sel_ready, 1)
            v.tensor_copy(LOG, logits).then_inc(sel_ready, 1)
            dve.wait_ge(sel_ready, 3)
            v.tensor_reduce(m12[:, 0, :], LOG, X_AXIS, ALU.max).then_inc(cur_ready, 1)
            dve.wait_ge(cur_ready, 1)
            v.tensor_tensor(EQ, LOG, wide(0), ALU.is_equal).then_inc(cur_ready, 1)
            dve.wait_ge(cur_ready, 2)
            v.tensor_tensor(SC, EQ, PRI, ALU.mult).then_inc(cur_ready, 1)
            dve.wait_ge(cur_ready, 3)
            link(v.tensor_reduce(m12[:, 4, :], SC, X_AXIS, ALU.max))
            link(v.tensor_tensor(F1, SC, wide(4), ALU.is_equal))
            link(v.scalar_tensor_tensor(L2, F1, -3.0e38, LOG, ALU.mult, ALU.add))
            link(v.tensor_reduce(m12[:, 1, :], L2, X_AXIS, ALU.max))
            link(v.tensor_tensor(EQ, L2, wide(1), ALU.is_equal))
            link(v.tensor_tensor(SC, EQ, PRI, ALU.mult))
            link(v.tensor_tensor(m12[:, 2, :], m12[:, 1, :], m12[:, 0, :], ALU.subtract))
            link(v.tensor_reduce(m12[:, 5, :], SC, X_AXIS, ALU.max))
            link(v.tensor_tensor(F2, SC, wide(5), ALU.is_equal))
            v.tensor_tensor(SEL, F1, F2, ALU.add).then_inc(sel_ready, 1)
            dve.wait_ge(ex_ready, 1)
            link(v.tensor_scalar(m12[:, 6, :], m12[:, 3, :], 1.0, None, ALU.add))
            link(v.reciprocal(m12[:, 6, :], m12[:, 6, :]))
            link(v.tensor_tensor(m12[:, 7, :], m12[:, 3, :], m12[:, 6, :], ALU.mult))
            link(v.tensor_tensor(COM, F1, wide(6), ALU.mult))
            link(v.tensor_tensor(TMP, F2, wide(7), ALU.mult))
            for c in range(2):
                v.tensor_tensor(combT[:, :, c * NE:c * NE + NE], COM, TMP, ALU.add).then_inc(route, 1)
            rt[0] += 2
            dve.wait_ge(*full(("rank",)))
            link(v.tensor_scalar(RNK, bank[1][:, 0:NT * NE].rearrange("p (t e) -> p t e", t=NT), 1.0, None, ALU.add))
            link(v.tensor_tensor(RNK, RNK, SEL, ALU.mult))
            link(v.tensor_scalar(slotT[:, :, 0:NE], RNK, -1.0, None, ALU.add))
            link(v.tensor_scalar(slotT[:, :, NE:2 * NE], RNK, -1.0 - P, None, ALU.add))
            link(v.memset(slotT[:, :, 2 * NE:2 * NE + 1], -1.0))
            dve.wait_ge(*full(("count",)))
            assert rt[0] == ROUTE_COUNT - 1
            link(v.tensor_reduce(cnts[:, 0:1], bank[2][:, 0:NE], X_AXIS, ALU.max))
            link(v.tensor_scalar(cnts[:, 1:2], cnts[:, 0:1], float(P), float(NE), ALU.is_gt, ALU.mult))
            v.tensor_scalar(n_it[:, :], cnts[0:1, 1:2], float(NE), None, ALU.add).then_inc(nit_ready, 1)

            def select(it, k):
                for t in range(NT):
                    ins = v.tensor_scalar(PM[:, t, :], iota[:, :], cur[:, 0, t:t + 1], None, ALU.is_equal)
                ins.then_inc(PM_ready, 1)

            v.tensor_copy(cur[:, 0, :], slotT[:, :, 0]).then_inc(cur_ready, 1)
            dve.wait_ge(cur_ready, 4)
            select(0, 0)

            v.memset(cnts[:, 2:3], 0.0).then_inc(zero_ready, 1)

            def gather_lo(banks, want):
                for b in banks:
                    dve.wait_ge(g_hi, want(b))
                    v.tensor_tensor(XL[:, 4 * b:4 * b + 4, 0:P],
                                    bank[5 + b][:, :].rearrange("p (c s) -> p c s", c=4),
                                    XH[:, 4 * b:4 * b + 4, 0:P].bitcast(F32), ALU.subtract).then_inc(g_lo, 1)
            gather_lo((0, 1), lambda b: b + 1)
            dve.sem_inc(y_lo, 2)
            dve.wait_ge(nit_ready, 1)
            n = dve.value_load(n_it[0:1, 0:1], min_val=NE, max_val=2 * NE)
            with dve.Fori(0, n) as it:
                def lo_m(i):
                    dve.wait_ge(hi_ready, it * NM + (NA + i + 1))
                    v.tensor_tensor(WL[:, (NA + i) % HL, :], raw[(i % NM) % RING_M],
                                    WH[:, (NA + i) % HL, :].bitcast(F32), ALU.subtract).then_inc(lo_ready, 1)

                def hT_lo_m(b):
                    dve.wait_ge(hT_hi, it * NB + (NB + b + 1))
                    v.tensor_tensor(hTl[:, 0, :], bank[2][:, 0:2 * P], hTh[:, 0, :].bitcast(F32),
                                    ALU.subtract).then_inc(hT_lo, 1)

                for i, (kind, j) in enumerate(moe):
                    lo_m(i + 2)
                    b = j // 2
                    if kind == "gu" and j % 2 == 0 and b >= 1:
                        hT_lo_m(b - 1)
                    if kind == "gu" and j % 2 == 1:
                        dve.wait_ge(silu_done, it * NB + (2 * NB + b + 1))
                        v.tensor_tensor(hh[:, 0, :], sg[:, 0, :], bank[b % 2][:, FB:2 * FB],
                                        ALU.mult).then_inc(h_ready, 1)
                    if kind == "gu" and j == 2 * 4 + 1:
                        dve.wait_ge(cur_ready, it * 2 + 4)
                        v.tensor_copy(cur[:, 0, :], slotT[:, :, bass.ds(it + 1, 1)].rearrange("p t o -> p (t o)")
                                      ).then_inc(cur_ready, 1)
                        v.tensor_copy(cur[:, 1, :], combT[:, :, bass.ds(it, 1)].rearrange("p t o -> p (t o)")
                                      ).then_inc(cur_ready, 1)
                    if kind == "gu" and j == 2 * 7 + 1:
                        dve.wait_ge(cur_ready, it * 2 + 6)
                        dve.wait_ge(PT_ready, it + 1)
                        select(it + 1, 0)
                    if kind == "down" and j == NB - 2:
                        hT_lo_m(NB - 1)
                        gather_lo((0,), lambda b: it * 2 + (2 + b + 1))
                    if kind == "down" and j == NB - 1:
                        for m in range(2):
                            dve.wait_ge(y_hi, it * 2 + (m + 1))
                            v.tensor_tensor(yl[:, m, :], bank[3 + m][:, :], yh[:, m, :].bitcast(F32),
                                            ALU.subtract).then_inc(y_lo, 1)
                        gather_lo((1,), lambda b: it * 2 + (2 + b + 1))
                        for r in range(4):
                            m, t = divmod(r, 2)
                            dve.wait_ge(*mfull(("scatter", r), it))
                            xv = xs[:, t, m * 512:m * 512 + 512]
                            v.scalar_tensor_tensor(xv, bank[SC_BANK[r]][:, :], cur[:, 1, t:t + 1], xv,
                                                   ALU.mult, ALU.add).then_inc(x_add, 1)

            N = norm_id("final", 0)
            norm_var(N)
            for m in range(2):
                dve.wait_ge(bank_full[m], n * per.used[m] + (base[m] + 1))
            for t in range(NT):
                for m in range(2):
                    ins = v.scalar_tensor_tensor(xn[:, t, m * 512:m * 512 + 512], xs[:, t, m * 512:m * 512 + 512],
                                                 rs[:, N, t:t + 1], bank[m][:, :], ALU.mult, ALU.mult)
                ins.then_inc(out_ready, 1)

        @block.tensor
        def _(pe):
            te = nc.tensor

            def claim(label):
                if plan.before[label]:
                    pe.wait_ge(*read(plan.before[label]))
                return bank[plan.of[label][0]]

            def done(ins, label):
                ins.then_inc(bank_full[plan.of[label][0]], 1)

            def mm3(out, ah, al, bh, bl, start, stop):
                te.matmul(out, ah, bh, start=start, stop=False)
                te.matmul(out, ah, bl, start=False, stop=False)
                return te.matmul(out, al, bh, start=False, stop=stop)

            def split(n):
                pe.wait_ge(lo_ready, n + 1)
                return WH[:, n % HL, :], WL[:, n % HL, :]

            def transposes(N, b, t_ready):
                label = ("norm", N, b)
                ps = claim(label)
                for c in range(2):
                    for t in range(NT):
                        if t_ready and b == 0 and c == 0:
                            pe.wait_ge(xn_ready, 2 * N + t + 1)
                        k = 2 * b + c
                        ins = te.transpose(ps[:, c * S + t * P:c * S + t * P + P], xn[:, t, k * P:k * P + P],
                                           ident[:, :])
                done(ins, label)

            def norm_T(kind, L):
                for b in range(4):
                    transposes(norm_id(kind, L), b, True)

            pe.wait_ge(c_id, 2)
            pe.wait_ge(c_one, 1)
            pe.wait_ge(rows_in, 16 * (8 + DEPTH))
            ps = claim(("vec",))
            te.transpose(ps[:, 0:VROWS], rows[0:VROWS, 0, :], ident[0:VROWS, 0:VROWS])
            R = TAPS * CC
            for L in range(DEPTH):
                ins = te.transpose(ps[:, P + L * R:P + L * R + R], rows[0:R, 1 + L, :], ident[0:R, 0:R])
            done(ins, ("vec",))
            norm_T("mix", 0)

            def feature_major(n, label, right_h, right_l, k_chunks, cols, ready=None):
                wh, wl = split(n)
                wh = wh.rearrange("p (k n) -> p k n", k=k_chunks)
                wl = wl.rearrange("p (k n) -> p k n", k=k_chunks)
                for ct in range(cols // P):
                    if ct % 2 == 0:
                        lab = label(ct // 2)
                        ps = claim(lab)
                    o = ps[:, (ct % 2) * S:(ct % 2) * S + S]
                    cs = slice(ct * P, ct * P + P)
                    for k in range(k_chunks):
                        if ready and ct == 0:
                            pe.wait_ge(*ready(k))
                        ins = mm3(o, wh[:, k, cs], wl[:, k, cs], right_h[:, k, :], right_l[:, k, :],
                                  k == 0, k == k_chunks - 1)
                    if ct % 2 == 1:
                        done(ins, lab)

            def token_major(n, kind, L, j, left_h, left_l):
                wh, wl = split(n)
                wh = wh.rearrange("p (k n) -> p k n", k=4)
                wl = wl.rearrange("p (k n) -> p k n", k=4)
                m, kh = divmod(j, 2)
                for t in range(NT):
                    label = (kind, L, m, t)
                    ps = claim(label) if kh == 0 else bk(label)
                    ts = slice(t * P, t * P + P)
                    for k in range(4):
                        kk = 4 * kh + k
                        ins = mm3(ps[:, :], left_h[:, kk, ts], left_l[:, kk, ts], wh[:, k, :], wl[:, k, :],
                                  kk == 0, kk == KC - 1)
                    if kh == 1:
                        done(ins, label)
                if kh == 0:
                    ins.then_inc(unit_used, 1)

            for n, (kind, L, j) in enumerate(units):
                if kind in ("a", "b", "pin", "gate"):
                    feature_major(n, lambda i: (kind, L, j), XH, XL, KC, 256, (kind, j) == ("a", 0) and
                                  (lambda k: (ht_lo, 4 * norm_id("mix", L) + k // 2 + 1)))
                    if L == 0 and (kind, j) == ("gate", 1):
                        norm_T("mem", 0)
                elif kind == "wpool":
                    pe.wait_ge(pooled_lo, 2 * L + 2)
                    wh, wl = split(n)
                    for b in range(4):
                        ps = claim((kind, L, b))
                        for c in range(2):
                            cs = slice(b * 256 + c * P, b * 256 + c * P + P)
                            ins = mm3(ps[:, c * S:c * S + S], wh[:, cs], wl[:, cs], SH[:, b, :], SL[:, b, :],
                                      True, True)
                        done(ins, (kind, L, b))
                elif kind == "k":
                    if j == 0:
                        pe.wait_ge(mT_lo, 8 * L + 8)
                    feature_major(n, lambda i: (kind, L, j), mTh, mTl, KC, 256)
                    if j == 3:
                        pe.wait_ge(conv_step, (L + 1) * TAPS * CC)
                        ps = claim(("mean", L))
                        for c in range(CC):
                            ins = te.matmul(ps[:, 0:S], ones[:, :], acc[:, c, :], start=(c == 0),
                                            stop=(c == CC - 1))
                        done(ins, ("mean", L))
                elif kind == "cout":
                    feature_major(n, lambda i: (kind, L, 2 * j + i), SH, SL, CC, 512,
                                  lambda k: (s_lo, CC * L + k + 1))
                elif kind == "mix":
                    pe.wait_ge(z_lo, 4 * L + (2 if j == 0 else 4))
                    token_major(n, kind, L, j, XH, XL)
                elif kind == "v":
                    token_major(n, kind, L, j, mTh, mTl)
                    if j == 0:
                        pe.wait_ge(csq_ready, L + 1)
                        ps = claim(("var", L))
                        for c in range(CC):
                            ins = te.matmul(ps[:, 0:S], ones[:, :], sqc[:, c, :], start=(c == 0),
                                            stop=(c == CC - 1))
                        done(ins, ("var", L))
                    if j == 2:
                        norm_T("xattn", L)
                elif kind == "q":
                    feature_major(n, lambda i: (kind, L, j), XH, XL, KC, 256, j == 0 and
                                  (lambda k: (ht_lo, 4 * norm_id("xattn", L) + k // 2 + 1)))
                elif kind == "xo":
                    if j == 0:
                        pe.wait_ge(o_lo, 4 * L + 4)
                    token_major(n, kind, L, j, XH, XL)
                elif kind == "gu":
                    b = j // 2
                    wh, wl = split(n)
                    wh = wh.rearrange("p (k n) -> p k n", k=4)
                    wl = wl.rearrange("p (k n) -> p k n", k=4)
                    for t in range(NT):
                        label = ("gu", L, b, t)
                        ps = claim(label) if j % 2 == 0 else bk(label)
                        ts = slice(t * P, t * P + P)
                        for k in range(4):
                            kk = 4 * (j % 2) + k
                            if b == 0 and t == 0:
                                pe.wait_ge(ht_lo, 4 * norm_id("ffn", L) + kk // 2 + 1)
                            ins = mm3(ps[:, :], XH[:, kk, ts], XL[:, kk, ts], wh[:, k, :], wl[:, k, :],
                                      kk == 0, kk == KC - 1)
                        if j % 2:
                            done(ins, label)
                    if j % 2 == 0:
                        ins.then_inc(unit_used, 1)
                elif kind == "down":
                    pe.wait_ge(hT_lo, j + 1)
                    wh, wl = split(n)
                    wh = wh.rearrange("p (k n) -> p k n", k=2)
                    wl = wl.rearrange("p (k n) -> p k n", k=2)
                    for t in range(NT):
                        for m in range(2):
                            label = ("ffn", L, m, t)
                            ps = claim(label) if j == 0 else bk(label)
                            for k in range(2):
                                ts = slice(t * P, t * P + P)
                                ms = slice(m * 512, m * 512 + 512)
                                ins = mm3(ps[:, :], hTh[:, k, ts], hTl[:, k, ts], wh[:, k, ms], wl[:, k, ms],
                                          j == 0 and k == 0, j == NB - 1 and k == 1)
                            if j == NB - 1:
                                done(ins, label)
                    if j < NB - 1:
                        ins.then_inc(unit_used, 1)
                    if j == NB - 1:
                        norm_T("mix", 1)
                hb = j // 2 if (kind == "gu" and j == 1) else j + 1 if (kind == "down" and j < NB - 1) else None
                if hb is not None:
                    label = ("hT", L, hb)
                    ps = claim(label)
                    for t in range(NT):
                        pe.wait_ge(h_ready, 2 * hb + t + 1)
                        for c in range(2):
                            ins = te.transpose(ps[:, c * S + t * P:c * S + t * P + P], hh[:, t, c * P:c * P + P],
                                               ident[:, :])
                    done(ins, label)
                if (kind, j) == ("q", 3):
                    pe.wait_ge(kT_ready, 4 * L + 4)
                    pe.wait_ge(qT_ready, 4 * L + 4)
                    for b in range(4):
                        t, hp = divmod(b, 2)
                        ps = claim(("score", L, b))
                        for hl in range(2):
                            h = 2 * hp + hl
                            for k in range(2):
                                ins = te.matmul(ps[:, hl * S:hl * S + S], qT[:, 2 * h + k, t * P:t * P + P],
                                                kT[:, 2 * h + k, :], start=(k == 0), stop=(k == 1))
                        done(ins, ("score", L, b))
                if (kind, j) == ("v", 3):
                    pe.wait_ge(p_norm, 8 * L + 8)
                    for h in range(NH):
                        ps = claim(("pT", L, h))
                        for mc in range(2):
                            for t in range(NT):
                                i = 4 * t + h
                                ins = te.transpose(ps[:, mc * S + t * P:mc * S + t * P + P],
                                                   prob[:, i, mc * P:mc * P + P], ident[:, :])
                        done(ins, ("pT", L, h))
                    pe.wait_ge(v_ready, 4 * L + 4)
                    for h in range(NH):
                        pe.wait_ge(pT_ready, 4 * L + h + 1)
                        ps = claim(("pv", L, h))
                        for dd in range(2):
                            for mc in range(2):
                                ins = te.matmul(ps[:, dd * S:dd * S + S],
                                                v_sb[:, mc, h * HD + dd * P:h * HD + dd * P + P],
                                                pT[:, 2 * h + mc, :], start=(mc == 0), stop=(mc == 1))
                        done(ins, ("pv", L, h))
                if (kind, j) == ("xo", 3):
                    if L == 1:
                        pe.wait_ge(grow_in, 16)
                        for m in range(2):
                            ps = claim(("gb", m))
                            done(te.matmul(ps[:, :], ones[0:1, :],
                                           sh[0:1, 2 * m:2 * m + 2, :].rearrange("p a b -> p (a b)"),
                                           start=True, stop=True), ("gb", m))
                    norm_T("ffn", L)

            pe.wait_ge(ht_lo, 4 * norm_id("ffn", 1) + 4)
            pe.wait_ge(wr_lo, 1)
            pe.wait_ge(router_in, 32)
            ps = claim(("logits",))
            for t in range(NT):
                ts = slice(t * P, t * P + P)
                o = ps[:, t * NE:t * NE + NE]
                te.matmul(o, ones[0:1, :], brow[0:1, :], start=True, stop=False)
                for k in range(KC):
                    ins = mm3(o, XH[:, k, ts], XL[:, k, ts], wrh[:, k, :], wrl[:, k, :], False, k == KC - 1)
            done(ins, ("logits",))
            pe.wait_ge(sel_ready, 4)
            sel = lg[:, 6]
            ps = claim(("rank",))
            te.matmul(ps[:, 0:NE], upper[:, :], sel[:, 0, :], start=True, stop=True)
            te.matmul(ps[:, NE:2 * NE], ones[:, :], sel[:, 0, :], start=True, stop=False)
            done(te.matmul(ps[:, NE:2 * NE], upper[:, :], sel[:, 1, :], start=False, stop=True), ("rank",))
            ps = claim(("count",))
            te.matmul(ps[:, 0:NE], ones[:, :], sel[:, 0, :], start=True, stop=False)
            done(te.matmul(ps[:, 0:NE], ones[:, :], sel[:, 1, :], start=False, stop=True), ("count",))

            def gather(b):
                for c in range(4):
                    k = 4 * b + c
                    o = bank[5 + b][:, c * P:c * P + P]
                    for i, (t, src) in enumerate(((0, xnh), (0, xnl), (1, xnh), (1, xnl))):
                        ins = te.matmul(o, src[:, t, k * P:k * P + P], PMr[:, t, :], start=(i == 0), stop=(i == 3))
                ins.then_inc(bank_full[5 + b], 1)

            pe.wait_ge(xnl_ready, NT)
            pe.wait_ge(PMr_ready, 1)
            for b in range(2):
                claim(("gather", b))
                gather(b)
            pe.wait_ge(nit_ready, 1)
            for b in (3, 4, 7):
                pe.wait_ge(*read(plan.last[b]))
            n = pe.value_load(n_it[0:1, 0:1], min_val=NE, max_val=2 * NE)
            with pe.Fori(0, n) as it:
                def claim_m(label):
                    prev = per.before[label]
                    back = prev is None
                    pe.wait_ge(*mread(prev or per.last[per.of[label][0]], back, it))
                    return bank[per.of[label][0]]

                def done_m(ins, label):
                    ins.then_inc(bank_full[per.of[label][0]], 1)

                def hT_m(b):
                    pe.wait_ge(h_ready, it * NB + (2 * NB + b + 1))
                    ps = claim_m(("hT", b))
                    for c in range(2):
                        ins = te.transpose(ps[:, c * P:c * P + P], hh[:, 0, c * P:c * P + P], ident[:, :])
                    done_m(ins, ("hT", b))

                for i, (kind, j) in enumerate(moe):
                    if kind == "gu" and j == 0:
                        pe.wait_ge(g_lo, it * 2 + 2)
                    if kind == "down":
                        pe.wait_ge(hT_lo, it * NB + (NB + j + 1))
                    pe.wait_ge(lo_ready, it * NM + (NA + i + 1))
                    wh, wl = WH[:, (NA + i) % HL, :], WL[:, (NA + i) % HL, :]
                    if kind == "gu":
                        b = j // 2
                        wh = wh.rearrange("p (k n) -> p k n", k=4)
                        wl = wl.rearrange("p (k n) -> p k n", k=4)
                        ps = claim_m(("gu", b)) if j % 2 == 0 else bank[b % 2]
                        for k in range(4):
                            kk = 4 * (j % 2) + k
                            ins = mm3(ps[:, :], XH[:, kk, 0:P], XL[:, kk, 0:P], wh[:, k, :], wl[:, k, :],
                                      kk == 0, kk == KC - 1)
                        if j % 2:
                            done_m(ins, ("gu", b))
                        else:
                            ins.then_inc(unit_used, 1)
                    else:
                        wh = wh.rearrange("p (k n) -> p k n", k=2)
                        wl = wl.rearrange("p (k n) -> p k n", k=2)
                        for m in range(2):
                            ps = claim_m(("y", m)) if j == 0 else bank[3 + m]
                            ms = slice(m * 512, m * 512 + 512)
                            for k in range(2):
                                ks = slice(k * P, k * P + P)
                                ins = mm3(ps[:, :], hTh[:, 0, ks], hTl[:, 0, ks], wh[:, k, ms], wl[:, k, ms],
                                          j == 0 and k == 0, j == NB - 1 and k == 1)
                            if j == NB - 1:
                                done_m(ins, ("y", m))
                        if j < NB - 1:
                            ins.then_inc(unit_used, 1)
                    if kind == "gu" and j == 2:
                        ps = claim_m(("PT",))
                        for t in range(NT):
                            ins = te.transpose(ps[:, t * P:t * P + P], PM[:, t, :], ident[:, :])
                        done_m(ins, ("PT",))
                    if kind == "gu" and j % 2 == 0 and j:
                        hT_m(j // 2 - 1)
                    if kind == "down" and j == NB - 2:
                        hT_m(NB - 1)
                        pe.wait_ge(PMr_ready, it + 2)
                        claim_m(("gather", 0))
                        gather(0)
                claim_m(("gather", 1))
                gather(1)
                pe.wait_ge(PT_ready, it + 1)
                for r in range(4):
                    m, t = divmod(r, 2)
                    pe.wait_ge(y_lo, it * 2 + (2 + m + 1))
                    ps = claim_m(("scatter", r))
                    ts = slice(t * P, t * P + P)
                    te.matmul(ps[:, :], PT[:, ts], yh[:, m, :], start=True, stop=False)
                    done_m(te.matmul(ps[:, :], PT[:, ts], yl[:, m, :], start=False, stop=True), ("scatter", r))

            pe.wait_ge(gfin_in, 16)
            pe.wait_ge(h_ready, n * NB + 2 * NB)
            for m in range(2):
                te.matmul(bank[m][:, :], ones[0:1, :],
                          sh[0:1, 2 * m:2 * m + 2, :].rearrange("p a b -> p (a b)"),
                          start=True, stop=True).then_inc(bank_full[m], 1)


_INS = ["x", "mem", "g_mix", "w_in", "w_pool", "pool_scale", "w_dw", "b_dw", "conv_ln_g", "conv_ln_b",
        "w_conv_out", "w_mix_out", "g_xattn", "g_mem", "w_xq", "w_xkv", "w_xo", "g_ffn", "w_ffn_gu",
        "w_ffn_down", "w_router", "b_router", "w_moe_gu", "w_moe_down", "g_final"]


def kernel(**inputs):
    import numpy as np
    import concourse.bacc as bacc
    from concourse.bass_utils import run_bass_kernel_spmd

    nc = bacc.Bacc("TRN2", target_bir_lowering=False, num_devices=1)
    arrays, args = {}, []
    for name in _INS:
        a = np.ascontiguousarray(inputs[name])
        arrays[f"in_{name}"] = a
        args.append(nc.dram_tensor(f"in_{name}", a.shape, mybir.dt.from_np(a.dtype), kind="ExternalInput").ap())
    out = nc.dram_tensor("out", inputs["x"].shape, F32, kind="ExternalOutput").ap()
    trunk(nc, *args, out)
    r = run_bass_kernel_spmd(nc, [arrays], core_ids=[0])
    return r.results[0]["out"]
```

```python
from contextlib import ExitStack

import concourse.bass as bass
from concourse import mybir


F32 = mybir.dt.float32
F32R = mybir.dt.float32r
I32 = mybir.dt.int32
ALU = mybir.AluOpType
ACT = mybir.ActivationFunctionType
X_AXIS = mybir.AxisListType.X

P = 128
EPS = 1e-6
UNIT = 2048
RING_A = 4
RING_M = 11
HL = 3


class BankPlan:

    def __init__(self):
        self.used = [0] * 8
        self.of = {}
        self.before = {}
        self.last = [None] * 8

    def add(self, label, bank):
        self.used[bank] += 1
        assert label not in self.of, label
        self.of[label] = (bank, self.used[bank])
        self.before[label], self.last[bank] = self.last[bank], label


def stream_plan(depth, n_blocks):
    units = []
    for L in range(depth):
        units += [("a", L, 0), ("b", L, 0), ("a", L, 1), ("b", L, 1), ("pin", L, 0), ("pin", L, 1)]
        units += [("gate", L, j) for j in range(8)]
        units += [("wpool", L, 0)]
        units += [("k", L, j) for j in range(4)]
        units += [("v", L, j) for j in range(3)]
        units += [("cout", L, j) for j in range(2)]
        units += [("mix", L, j) for j in range(4)]
        units += [("q", L, j) for j in range(4)]
        units += [("v", L, 3)]
        units += [("xo", L, j) for j in range(4)]
        if L % 2 == 0:
            units += ffn_units(L, n_blocks)
    return units


def ffn_units(L, n_blocks):
    units = []
    for b in range(n_blocks):
        units += [("gu", L, 2 * b), ("gu", L, 2 * b + 1)]
        if b:
            units += [("down", L, b - 1)]
    return units + [("down", L, n_blocks - 1)]


def trunk(nc, x, mem, g_mix, w_in, w_pool, pool_scale, w_dw, b_dw, conv_ln_g, conv_ln_b, w_conv_out,
          w_mix_out, g_xattn, g_mem, w_xq, w_xkv, w_xo, g_ffn, w_ffn_gu, w_ffn_down, w_router,
          b_router, w_moe_gu, w_moe_down, g_final, out):
    DEPTH, D = g_mix.shape
    S = x.shape[1]
    KC = D // P
    NT = S // P
    CW = w_dw.shape[3]
    CC = CW // P
    TAPS = w_dw.shape[1]
    PAD = TAPS - 1
    WINDOWS = (2, 4, 8, 16)
    PPAD = max(WINDOWS)
    NH = 4
    HD = D // NH
    FF = w_ffn_down.shape[1]
    FB = 256
    NB = FF // FB
    NE = w_moe_gu.shape[1]
    VROWS = 4 * DEPTH * KC + DEPTH * KC + 3 * DEPTH * CC
    assert (D, S, CW, DEPTH, NE) == (1024, 256, 512, 2, 8) and NB * FB == FF and VROWS <= P

    units = stream_plan(DEPTH, NB)
    NA = len(units)
    index = {u: n for n, u in enumerate(units)}
    moe = [(kind, i) for kind, _, i in ffn_units(1, NB)]
    NM = len(moe)
    assert NM % RING_M == 0 and NM % HL == 0

    plan = BankPlan()
    plan.add(("vec",), 0)
    def norm_id(kind, L):
        return {"mix": (0, 4), "mem": (1, 1), "xattn": (2, 5), "ffn": (3, 6), "final": (7, 7)}[kind][L]
    def plan_norm(kind, L, at=(4, 5, 6, 7), pieces=range(4)):
        for b in pieces:
            plan.add(("norm", norm_id(kind, L), b), at[b])
    V_BANK, COUT_BANK, MIX_BANK = (6, 0), 2, (6, 4)
    plan_norm("mix", 0)
    for (kind, L, j) in units:
        if kind in ("a", "b"):
            plan.add((kind, L, j), 2 * j + (kind == "b"))
        elif kind == "pin":
            plan.add((kind, L, j), j)
        elif kind == "gate":
            plan.add((kind, L, j), (2 + j) % 4)
        elif kind == "wpool":
            for b in range(4):
                plan.add((kind, L, b), b)
        elif kind == "k":
            plan.add((kind, L, j), 4 + j)
        elif kind == "cout":
            for b in (2 * j, 2 * j + 1):
                plan.add((kind, L, b), COUT_BANK + b)
        elif kind in ("mix", "xo") and j % 2 == 0:
            for t in range(NT):
                plan.add((kind, L, j // 2, t), (MIX_BANK[j // 2] if kind == "mix" else j) + t)
        elif kind == "v" and j % 2 == 0:
            for t in range(NT):
                plan.add((kind, L, j // 2, t), V_BANK[j // 2] + t)
        elif kind == "q":
            plan.add((kind, L, j), 2 + j % 2)
        elif kind == "gu" and j % 2 == 0:
            for t in range(NT):
                plan.add(("gu", L, j // 2, t), t)
        if (kind, L, j) == ("b", 0, 0):
            plan_norm("mem", 0)
        if (kind, j) == ("v", 0):
            plan.add(("mean", L), 4)
        if (kind, j) == ("v", 1):
            plan.add(("var", L), 5)
        if (kind, j) in (("mix", 2), ("q", 0)):
            plan_norm("xattn", L, (6, 7, 4, 5), (0, 1) if kind == "mix" else (2, 3))
        if (kind, j) == ("xo", 2):
            plan_norm("ffn", L, pieces=(0, 1))
        if (kind, L, j) in (("xo", 1, 3), ("gu", 0, 0)):
            plan_norm("ffn", L, pieces=(2, 3))
        if (kind, j) == ("q", 3):
            for b in range(4):
                plan.add(("score", L, b), 4 + b)
        if (kind, j) == ("v", 3):
            for b in range(4):
                plan.add(("pT", L, b), b)
            for b in range(4):
                plan.add(("pv", L, b), 4 + b)
        if kind == "gu" and j % 2 == 1:
            plan.add(("hT", L, j // 2), 2)
            if j == 1:
                for t in range(NT):
                    for n in range(2):
                        plan.add(("ffn", L, n, t), 4 + 2 * n + t)
        if kind == "down" and j == NB - 1:
            plan_norm("mix", 1)
    plan.add(("logitsT",), 0)
    plan.add(("logits",), 5)
    plan.add(("rank",), 2)
    plan.add(("count",), 3)
    GATHER_BANK = (5, 6, 0, 1)
    for b in range(4):
        plan.add(("gather", b), GATHER_BANK[b])
    base = list(plan.used)
    per = BankPlan()
    for b in range(NB):
        per.add(("gu", b), b % 2)
        if b == 1:
            per.add(("PT",), 7)
        if b:
            per.add(("hT", b - 1), 2)
        if b == 1:
            per.add(("y", 0), 3)
            per.add(("y", 1), 4)
    per.add(("hT", NB - 1), 2)
    for b in range(4):
        per.add(("gather", b), GATHER_BANK[b])
    SC_BANK = (7, 2, 5, 6)
    for r in range(4):
        per.add(("scatter", r), SC_BANK[r])

    with ExitStack() as ctx:
        def sb(name, shape, dt=F32):
            return ctx.enter_context(nc.sbuf_tensor(name, shape, dt))

        def sem(name):
            return ctx.enter_context(nc.semaphore(name))

        bank = [ctx.enter_context(nc.psum_tensor(f"bank{b}", [P, 512], F32)) for b in range(8)]
        bank_full = [sem(f"bank_full{b}") for b in range(8)]

        arena = sb("arena", [P, RING_M * UNIT])
        raw = [arena[:, s * UNIT:(s + 1) * UNIT] for s in range(RING_M)]
        at = RING_A * UNIT
        def carve(n):
            nonlocal at
            at += n
            assert at <= RING_M * UNIT
            return arena[:, at - n:at]
        gate_b = carve(16 * S)
        gates = gate_b.rearrange("p (c s) -> p c s", s=S)
        qT = gates[:, 0:8, :]
        prob = gates[:, 8:16, :]
        kv_b = carve(16 * S)
        kT = kv_b[:, 0:8 * S].rearrange("p (c s) -> p c s", s=S)
        pT = kT
        v_sb = kv_b[:, 8 * S:16 * S].rearrange("p (t d) -> p t d", t=NT)
        mem_b = carve(8 * S)
        memT = mem_b.rearrange("p (c s) -> p c s", s=S)
        mem_in = mem_b.rearrange("p (t d) -> p t d", t=NT)
        cu_b = carve(CC * (PAD + S))
        cu = cu_b.rearrange("p (c s) -> p c s", c=CC)
        pu_b = carve(CC * (PPAD + S))
        pu = pu_b.rearrange("p (c s) -> p c s", c=CC)
        W1, W2 = CC * (PPAD + S), (CC - 1) * (PPAD + S)
        assert W1 + W2 <= 8 * S
        s1 = kv_b[:, 8 * S:8 * S + W1].rearrange("p (c s) -> p c s", c=CC)
        s2 = kv_b[:, 8 * S + W1:8 * S + W1 + W2].rearrange("p (c s) -> p c s", c=CC - 1)
        acc_b = carve(CC * S)
        acc = acc_b.rearrange("p (c s) -> p c s", c=CC)
        sqc = cu[:, :, PAD:PAD + S]
        sgc = pu[:, :, PPAD:PPAD + S]
        rows = gate_b[:, 0:3 * P].rearrange("p (r n) -> p r n", r=3)

        WH = sb("WH", [P, HL, UNIT], F32R)
        WL = sb("WL", [P, HL, UNIT], F32R)
        xs = sb("xs", [P, NT, D])
        xn = sb("xn", [P, NT, D])
        XH = sb("XH", [P, KC, S], F32R)
        XL = sb("XL", [P, KC, S], F32R)
        MH = sb("MH", [P, KC * S], F32R)
        ML = sb("ML", [P, KC * S], F32R)
        mTh = MH[:, :].rearrange("p (c s) -> p c s", s=S)
        mTl = ML[:, :].rearrange("p (c s) -> p c s", s=S)
        xnh = MH[:, :].rearrange("p (t d) -> p t d", t=NT)
        xnl = ML[:, :].rearrange("p (t d) -> p t d", t=NT)
        SH = sb("SH", [P, CC, S], F32R)
        SL = sb("SL", [P, CC, S], F32R)
        yh = SH[:, :, :].rearrange("p (n a) s -> p n (a s)", n=2)
        yl = SL[:, :, :].rearrange("p (n a) s -> p n (a s)", n=2)
        sh = sb("sh", [P, 4, FB])
        sg = sh[:, 0:2, :]
        hh = sh[:, 2:4, :]
        gain_rows = sh[:, :, :].rearrange("p a b -> p (a b)")
        PM = sh[:, 3, :].rearrange("p (t s) -> p t s", t=NT)
        hTh = sb("hTh", [P, 2, S], F32R)
        hTl = sb("hTl", [P, 2, S], F32R)
        PMr = hTh[:, 1, :].rearrange("p (t s) -> p t s", t=NT)
        PT = hTl[:, 1, :]
        ident = sb("ident", [P, P])
        upper = sb("upper", [P, P])
        ones = sb("ones", [P, P])
        iota = sb("iota", [P, P])
        vec = sb("vec", [P, VROWS + DEPTH * TAPS * CC])
        icnt = sb("icnt", [P, CC, PPAD])
        m16 = sb("m16", [P, CC, PPAD])
        ss = sb("ss", [P, 8, NT, 2])
        mhalf = sb("mhalf", [P, NT])
        vv = sb("vv", [P, 8, NT])
        rs = sb("rs", [P, 8, NT])
        wr = sb("wr", [P, KC, NE])
        wrh = sb("wrh", [P, KC, NE], F32R)
        wrl = sb("wrl", [P, KC, NE], F32R)
        brow = sb("brow", [1, NE])
        bias = sb("bias", [P, NE])
        lgT = sb("lgT", [NE, S])
        rq = sb("rq", [P, NT])
        unused = sb("unused", [P, 4])
        lg = sb("lg", [P, 9, NT, NE])
        LOG, F1, L2, F2, SEL, COM, TMP, PRI, SC = (lg[:, i] for i in range(9))
        m12 = sb("m12", [P, 8, NT])
        slotT = sb("slotT", [P, NT, 2 * NE + 1])
        combT = sb("combT", [P, NT, 2 * NE])
        cur = sb("cur", [P, 2, NT])
        cnts = sb("cnts", [P, 4])
        n_it = sb("n_it", [1, 1], I32)
        smx = sb("smx", [P, 3, 8])

        GC = {"mix": 0, "xattn": DEPTH * KC, "mem": 2 * DEPTH * KC, "ffn": 3 * DEPTH * KC}
        PS0 = 4 * DEPTH * KC
        BD0 = PS0 + DEPTH * KC
        LG0 = BD0 + DEPTH * CC
        LB0 = LG0 + DEPTH * CC

        def gcol(kind, L, c):
            return vec[:, GC[kind] + L * KC + c:GC[kind] + L * KC + c + 1]

        def col(at0, L, width, c):
            return vec[:, at0 + L * width + c:at0 + L * width + c + 1]

        def tap(L, k, c):
            o = VROWS + (L * TAPS + k) * CC + c
            return vec[:, o:o + 1]

        raw_landed = [sem(f"raw_landed{s}") for s in range(RING_M)]
        hi_ready, lo_ready, unit_used = sem("hi_ready"), sem("lo_ready"), sem("unit_used")
        x_in = [sem(f"x_in{t}") for t in range(NT)]
        mem_in_s, rows_in, router_in, grow_in, gfin_in = (sem(n) for n in (
            "mem_landed", "rows_in", "router_in", "grow_in", "gfin_in"))
        c_id0, c_id, c_one, c_iota, c_cnt0, c_cnt, c_pad, vec_ready = (sem(n) for n in (
            "const_zeroed", "const_ident", "const_ones", "const_iota", "count_iota", "count_ready",
            "pads_zero", "vec_ready"))
        c_half = sem("const_minus_half")
        sq_done, var_ready, rstd_ready, xn_ready, ht_hi, ht_lo = (sem(n) for n in (
            "sq_done", "var_ready", "rstd_ready", "xn_ready", "ht_hi", "ht_lo"))
        mT_hi, mT_lo, sig_b, cu_ready, gate_ready, pu_ready = (sem(n) for n in (
            "mT_hi", "mT_lo", "sig_b", "cu_ready", "gate_ready", "pu_ready"))
        pool_step, pooled_hi, pooled_lo, zp_ready, conv_step = (sem(n) for n in (
            "pool_step", "pooled_hi", "pooled_lo", "zpool_ready", "conv_step"))
        cen_ready, csq_ready, cvar, cstd, crstd, cnorm, csilu, s_hi, s_lo = (sem(n) for n in (
            "conv_centred", "conv_squared", "conv_var", "conv_std", "conv_rstd", "conv_normed", "conv_silu",
            "s_hi", "s_lo"))
        zc_ready, z_ready, z_hi, z_lo, x_add, kT_ready, v_ready, qT_ready = (sem(n) for n in (
            "zc_ready", "z_ready", "z_hi", "z_lo", "x_add", "kT_ready", "v_ready", "qT_ready"))
        mx_ready, nmx_ready, p_exp, rden, p_norm, pT_ready, o_hi, o_lo = (sem(n) for n in (
            "mx_ready", "nmx_ready", "p_exp", "rden", "p_norm", "pT_ready", "o_hi", "o_lo"))
        silu_done, h_ready, hT_hi, hT_lo = (sem(n) for n in ("silu_done", "h_ready", "hT_hi", "hT_lo"))
        tab_ready, xnh_ready, xnl_ready, wr_hi, wr_lo, route, ex_ready, sel_ready = (sem(n) for n in (
            "table_ready", "xnh_ready", "xnl_ready", "wr_hi", "wr_lo", "route", "ex_ready", "sel_ready"))
        zero_ready, rq_ready, lgT_ready = sem("zero_ready"), sem("rq_ready"), sem("lgT_ready")
        nit_ready, cur_ready, PM_ready, PMr_ready, PT_ready, g_hi, g_lo, y_hi, y_lo, out_ready, stored = (
            sem(n) for n in ("nit_ready", "cur_ready", "PM_ready", "PMr_ready", "PT_ready", "gather_hi",
                             "gather_lo", "y_hi", "y_lo", "out_ready", "stored"))

        ROUTE_DIFF, ROUTE_RANK, ROUTE_COUNT = 10, 13, 16
        POOL_STEPS = 2 + 5 * CC

        def full(label):
            b, k = plan.of[label]
            return bank_full[b], k

        def mfull(label, it):
            b, k = per.of[label]
            return bank_full[b], it * per.used[b] + (base[b] + k)

        def bk(label):
            return bank[(plan.of.get(label) or per.of.get(label))[0]]

        def last_result(kind, L, j):
            if kind in ("a", "b", "pin", "gate", "k", "q"):
                return (kind, L, j)
            if kind == "wpool":
                return (kind, L, 3)
            if kind == "cout":
                return (kind, L, 2 * j + 1)
            if kind in ("mix", "xo", "v") and j % 2:
                return (kind, L, j // 2, NT - 1)
            if kind == "gu" and j % 2:
                return (kind, L, j // 2, NT - 1)
            if kind == "down" and j == NB - 1:
                return ("ffn", L, 1, NT - 1)
            return None

        n_used, used_at = 0, []
        for u in units:
            n_used += last_result(*u) is None
            used_at.append(n_used)
        used_base, n_used, moe_used = n_used, 0, []
        for (kind, j) in moe:
            n_used += (kind == "gu" and j % 2 == 0) or (kind == "down" and j < NB - 1)
            moe_used.append(n_used)
        used_per = n_used

        def through(n):
            label = last_result(*units[n])
            return full(label) if label else (unit_used, used_at[n])

        def mthrough(i, it):
            off, (kind, j) = i // NM, moe[i % NM]
            label = ("gu", j // 2) if kind == "gu" and j % 2 else ("y", 1) if (kind, j) == ("down", NB - 1) else None
            if label:
                b, k = per.of[label]
                return bank_full[b], it * per.used[b] + (off * per.used[b] + base[b] + k)
            return unit_used, it * used_per + (off * used_per + used_base + moe_used[i % NM])

        XN = {("mix", 0): 0, ("mem", 0): 1, ("mix", 1): 2, ("ffn", 1): 3}

        def xadd(L, stage, i):
            return 12 * L + {"mix": 0, "xo": 4, "ffn": 8}[stage] + i + 1

        def read(label):
            kind, *r = label
            if kind == "vec":
                return vec_ready, 1
            if kind == "norm":
                N, b = r
                return (ht_hi if N == norm_id("mem", 0) else ht_lo), 4 * N + b + 1
            if kind == "logitsT":
                return lgT_ready, 1
            if kind in ("logits", "rank", "count", "gather"):
                return {"logits": (sel_ready, 4),
                        "rank": (route, ROUTE_RANK), "count": (route, ROUTE_COUNT),
                        "gather": (g_lo, r[0] + 1 if r else 0)}[kind]
            L = r[0]
            if kind in ("mix", "xo", "ffn"):
                return x_add, xadd(L, kind, 2 * r[1] + r[2] if kind != "ffn" else 2 * r[2] + r[1])
            return {
                "a": lambda j: (cu_ready, 2 * L + j + 1),
                "b": lambda j: (sig_b, 2 * L + j + 1),
                "pin": lambda j: (pu_ready, 2 * L + j + 1),
                "gate": lambda j: (gate_ready, 8 * L + j + 1),
                "wpool": lambda b: (zp_ready, 8 * L + 2 * b + 2),
                "k": lambda j: (kT_ready, 4 * L + j + 1),
                "mean": lambda: (cen_ready, L + 1),
                "var": lambda: (cvar, L + 1),
                "cout": lambda b: (zc_ready, 4 * L + b + 1),
                "v": lambda m, t: (v_ready, 4 * L + 2 * m + t + 1),
                "q": lambda j: (qT_ready, 4 * L + j + 1),
                "score": lambda b: (p_exp, 8 * L + 2 * b + 2),
                "pT": lambda h: (pT_ready, 4 * L + h + 1),
                "pv": lambda h: (o_lo, 4 * L + h + 1),
                "gu": lambda b, t: (h_ready, 2 * b + t + 1),
                "hT": lambda b: (hT_lo, b + 1),
            }[kind](*r[1:])

        def mread(label, back, it):
            kind, *r = label
            s, n, k = {
                "gu": lambda b: (h_ready, NB, 2 * NB + b + 1),
                "hT": lambda b: (hT_lo, NB, NB + b + 1),
                "PT": lambda: (PT_ready, 1, 1),
                "y": lambda m: (y_lo, 2, 2 + m + 1),
                "gather": lambda b: (g_lo, 4, 4 + b + 1),
                "scatter": lambda q: (x_add, 4, xadd(1, "ffn", q)),
            }[kind](*r)
            return s, it * n + (k - n * back)

        def wsrc(kind, L, j):
            if kind in ("a", "b", "pin", "gate"):
                c0 = {"pin": 0, "a": CW, "b": 2 * CW, "gate": 3 * CW}[kind] + j * 256
                return w_in[L].rearrange("(k p) n -> p k n", p=P)[:, :, c0:c0 + 256]
            if kind in ("k", "q"):
                w = w_xkv if kind == "k" else w_xq
                return w[L].rearrange("(k p) n -> p k n", p=P)[:, :, j * 256:j * 256 + 256]
            if kind == "wpool":
                return w_pool[L].rearrange("g p n -> p g n")
            if kind == "cout":
                return w_conv_out[L].rearrange("(k p) n -> p k n", p=P)[:, :, j * 512:j * 512 + 512]
            if kind in ("mix", "xo", "v"):
                w = {"mix": w_mix_out, "xo": w_xo, "v": w_xkv}[kind]
                c0 = (D if kind == "v" else 0) + (j // 2) * 512
                return w[L].rearrange("(k p) n -> p k n", p=P)[:, 4 * (j % 2):4 * (j % 2) + 4, c0:c0 + 512]
            if kind == "gu":
                return gu_src(w_ffn_gu[L // 2], j)
            return w_ffn_down[L // 2].rearrange("(b k p) n -> b p k n", k=2, p=P)[j]

        def gu_src(w, j):
            v = w.rearrange("(k p) (s f) -> p k s f", p=P, s=2)
            return v[:, 4 * (j % 2):4 * (j % 2) + 4, :, (j // 2) * FB:(j // 2) * FB + FB]

        def wdst(kind, slot):
            r = raw[slot]
            if kind in ("a", "b", "pin", "gate", "k", "q"):
                return r.rearrange("p (k n) -> p k n", k=8)
            if kind == "wpool":
                return r[:, 0:1024].rearrange("p (g n) -> p g n", g=4)
            if kind == "gu":
                return r.rearrange("p (k s f) -> p k s f", k=4, s=2)
            if kind == "down":
                return r.rearrange("p (k n) -> p k n", k=2)
            return r.rearrange("p (k n) -> p k n", k=4)

        def gathered(b):
            return bank[GATHER_BANK[b]][:, :].rearrange("p (c s) -> p c s", c=2)[:, :, 0:P]

        def width(n):
            return 1024 if n < NA and units[n][0] == "wpool" else UNIT

        block = ctx.enter_context(nc.Block())

        @block.sync
        def _(sp):
            for t in range(NT):
                sp.dma_start(xs[:, t, :], x[0].rearrange("(t p) d -> p t d", p=P)[:, t]).then_inc(x_in[t], 16)
            sp.dma_start(wdst("a", 0), wsrc(*units[0])).then_inc(raw_landed[0], 16)
            r = 0
            for src in (g_mix, g_xattn, g_mem, g_ffn, pool_scale, b_dw, conv_ln_g, conv_ln_b):
                v = src.rearrange("l (k p) -> (l k) p", p=P)
                sp.dma_start(rows[r:r + v.shape[0], 0, :], v).then_inc(rows_in, 16)
                r += v.shape[0]
            sp.dma_start(rows[0:TAPS * CC, 1:1 + DEPTH, :],
                         w_dw.rearrange("l k o (c p) -> (k o c) l p", p=P)).then_inc(rows_in, 16)
            sp.dma_start(brow[:, :], b_router).then_inc(rows_in, 16)
            for n, (kind, L, j) in list(enumerate(units))[1:]:
                if n >= RING_A:
                    sp.wait_ge(lo_ready, n - RING_A + 1)
                dst, src = wdst(kind, n % RING_A), wsrc(kind, L, j)
                if kind == "gu":
                    for s in range(2):
                        sp.dma_start(dst[:, :, s, :], src[:, :, s, :]).then_inc(raw_landed[n % RING_A], 16)
                else:
                    sp.dma_start(dst, src).then_inc(raw_landed[n % RING_A], 16)

            def load_expert_unit(e, i):
                kind, j = moe[i]
                s = i % RING_M
                dst = wdst(kind, s)
                if kind == "gu":
                    w = w_moe_gu[0].rearrange("e (k p) (s f) -> e p k s f", p=P, s=2)
                    k0, f0 = 4 * (j % 2), (j // 2) * FB
                    for h in range(2):
                        src = w[bass.ds(e, 1), :, k0:k0 + 4, h, f0:f0 + FB].rearrange("o p k f -> (o p) k f")
                        sp.dma_start(dst[:, :, h, :], src).then_inc(raw_landed[s], 16)
                else:
                    w = w_moe_down[0].rearrange("e (b k p) n -> e b p k n", k=2, p=P)
                    src = w[bass.ds(e, 1), j].rearrange("o p k n -> (o p) k n")
                    sp.dma_start(dst, src).then_inc(raw_landed[s], 16)

            last_dense = {i: max(n for n in range(NA) if n % RING_A == i) for i in range(RING_A)}
            for i in (0, 3, 1, 4, 5, 2, *range(6, RING_M)):
                if i < RING_A:
                    sp.wait_ge(lo_ready, last_dense[i] + 1)
                elif i == RING_A:
                    sp.wait_ge(s_lo, CC * DEPTH)
                    sp.wait_ge(o_lo, 4 * DEPTH)
                load_expert_unit(0, i)
            for i in range(RING_M, NM):
                sp.wait_ge(lo_ready, NA + i - RING_M + 1)
                load_expert_unit(0, i)
            sp.wait_ge(nit_ready, 1)
            n = sp.value_load(n_it[0:1, 0:1], min_val=NE, max_val=2 * NE)
            with sp.Fori(1, n) as it:
                for i in range(NM):
                    sp.wait_ge(lo_ready, it * NM + (NA + i - RING_M + 1))
                    load_expert_unit(it % NE, i)
            for i in range(2):
                sp.wait_ge(lo_ready, n * NM + (NA + i - RING_M + 1))
                sp.sem_inc(raw_landed[i], 32)
            for t in range(NT):
                sp.wait_ge(out_ready, t + 1)
                sp.dma_start(out[0].rearrange("(t p) d -> p t d", p=P)[:, t], xn[:, t]).then_inc(stored, 16)
            sp.wait_ge(stored, 16 * NT)

        LANDS = {"gu": 32}

        landed = [0] * RING_M
        dense_landed = []
        for n, (kind, L, j) in enumerate(units):
            landed[n % RING_A] += LANDS.get(kind, 16)
            dense_landed.append(landed[n % RING_A])
        landed_base = list(landed)
        moe_landed, per_slot = [], [0] * RING_M
        for i, (kind, j) in enumerate(moe):
            per_slot[i % RING_M] += LANDS.get(kind, 16)
            moe_landed.append(per_slot[i % RING_M])

        @block.gpsimd
        def _(pool):
            g = nc.gpsimd
            g.memset(ident[:, :], 0.0).then_inc(c_id0, 1)
            g.memset(upper[:, :], 1.0).then_inc(c_id0, 1)
            g.memset(ones[:, :], 1.0).then_inc(c_one, 1)
            pool.wait_ge(c_id0, 2)
            g.affine_select(out=ident[:, :], in_=ident[:, :], compare_op=ALU.not_equal, fill=1.0, base=0,
                            pattern=[[-1, P]], channel_multiplier=1).then_inc(c_id, 1)
            g.affine_select(out=upper[:, :], in_=upper[:, :], compare_op=ALU.is_gt, fill=0.0, base=0,
                            pattern=[[1, P]], channel_multiplier=-1).then_inc(c_id, 1)
            g.iota(iota[:, :], pattern=[[1, P]], base=1, channel_multiplier=0,
                   allow_small_or_imprecise_dtypes=True).then_inc(c_iota, 1)
            g.iota(m16[:, :, :], pattern=[[0, CC], [1, PPAD]], base=1, channel_multiplier=0,
                   allow_small_or_imprecise_dtypes=True).then_inc(c_cnt0, 1)
            g.memset(cu[:, :, 0:PAD], 0.0).then_inc(c_pad, 1)
            g.memset(pu[:, :, 0:PPAD], 0.0).then_inc(c_pad, 1)
            pool.wait_ge(c_cnt0, 1)
            for c, w in enumerate(WINDOWS):
                g.tensor_scalar(m16[:, c, :], m16[:, c, :], float(w), None, ALU.min).then_inc(c_cnt0, 1)
            g.memset(mhalf[:, :], -0.5).then_inc(c_half, 1)
            pool.wait_ge(c_half, 1)

            def rstd(N):
                pool.wait_ge(var_ready, N + 1)
                g.tensor_tensor(rs[:, N, :], vv[:, N, :], mhalf[:, :], ALU.pow).then_inc(rstd_ready, 1)

            rstd(norm_id("mix", 0))
            rstd(norm_id("mem", 0))
            for L in range(DEPTH):
                o = L * POOL_STEPS
                pool.wait_ge(pu_ready, 2 * L + 2)
                if L:
                    pool.wait_ge(o_lo, 4 * L)
                g.memset(s1[:, :, 0:PPAD], 0.0).then_inc(pool_step, 1)
                g.memset(s2[:, :, 0:PPAD], 0.0).then_inc(pool_step, 1)
                views = ((pu, 0), (s1, 0), (s2, 1), (s1, 0), (s2, 1))
                for i in range(CC):
                    lag = 1 << i
                    (src, s0), (dst, d0) = views[i], views[i + 1]
                    pool.wait_ge(pool_step, o + 2 + i)
                    g.tensor_tensor(dst[:, i - d0:CC - d0, PPAD:PPAD + S], src[:, i - s0:CC - s0, PPAD:PPAD + S],
                                    src[:, i - s0:CC - s0, PPAD - lag:PPAD + S - lag],
                                    ALU.add).then_inc(pool_step, 1)
                pool.wait_ge(pool_step, o + 2 + CC)
                pool.wait_ge(c_cnt, 1)
                for c in range(CC):
                    w, w0 = views[c + 1]
                    g.tensor_tensor(m16[:, c, :], w[:, c - w0, PPAD:2 * PPAD], icnt[:, c, :],
                                    ALU.mult).then_inc(pool_step, 1)
                    g.tensor_scalar(w[:, c - w0, 2 * PPAD:], w[:, c - w0, 2 * PPAD:], 1.0 / WINDOWS[c], None,
                                    ALU.mult).then_inc(pool_step, 1)
                pool.wait_ge(pool_step, o + 2 + 3 * CC)
                for c in range(CC):
                    w, w0 = views[c + 1]
                    g.tensor_tensor(w[:, c - w0, PPAD:2 * PPAD], m16[:, c, :], pu[:, c, PPAD:2 * PPAD],
                                    ALU.subtract).then_inc(pool_step, 1)
                    g.tensor_tensor(w[:, c - w0, 2 * PPAD:], w[:, c - w0, 2 * PPAD:], pu[:, c, 2 * PPAD:],
                                    ALU.subtract).then_inc(pool_step, 1)
                rstd(norm_id("xattn", L))
                rstd(norm_id("ffn", L))
                if L == 0:
                    rstd(norm_id("mix", 1))
            rstd(norm_id("final", 0))

        @block.scalar
        def _(act):
            a = nc.scalar

            def hi(n):
                if n >= NA:
                    i = n - NA
                    act.wait_ge(raw_landed[i % RING_M], landed_base[i % RING_M] + moe_landed[i])
                else:
                    act.wait_ge(raw_landed[n % RING_A], dense_landed[n])
                if n >= HL:
                    act.wait_ge(*through(n - HL))
                s = raw[n % RING_A] if n < NA else raw[(n - NA) % RING_M]
                a.activation(WH[:, n % HL, 0:width(n)], s[:, 0:width(n)], ACT.Copy).then_inc(hi_ready, 1)

            def squares(N, src, pieces, ready):
                for i, (m, t) in enumerate(pieces):
                    act.wait_ge(*ready(i, t))
                    ms = slice(m * 512, m * 512 + 512)
                    a.activation(xn[:, t, ms], src[:, t, ms], ACT.Square, scale=D ** -0.5,
                                 accum_out=ss[:, N, t, m:m + 1]).then_inc(sq_done, 1)

            BY_HALF = [(m, t) for m in range(2) for t in range(NT)]
            BY_TILE = [(m, t) for t in range(NT) for m in range(2)]

            def norm_hi(kind, L, pieces=range(4)):
                N = norm_id(kind, L)
                for b in pieces:
                    act.wait_ge(*full(("norm", N, b)))
                    ps = bk(("norm", N, b))[:, :].rearrange("p (c s) -> p c s", c=2)
                    for c in range(2):
                        ins = a.activation(XH[:, 2 * b + c, :], ps[:, c, :], ACT.Copy,
                                           scale=gcol(kind, L, 2 * b + c))
                    ins.then_inc(ht_hi, 1)

            def x_squares(kind, L, stage, m):
                squares(norm_id(kind, L), xs, BY_HALF[2 * m:2 * m + 2],
                        lambda i, t: (x_add, xadd(L, stage, 2 * m + i)))

            def v_copies(L, m):
                for t in range(NT):
                    act.wait_ge(*full(("v", L, m, t)))
                    a.activation(v_sb[:, t, m * 512:m * 512 + 512], bk(("v", L, m, t))[:, :],
                                 ACT.Copy).then_inc(v_ready, 1)

            def copy_hi(out, in_, full_label, s):
                act.wait_ge(*full(full_label))
                a.activation(out, in_, ACT.Copy).then_inc(s, 1)

            squares(norm_id("mix", 0), xs, BY_TILE, lambda i, t: (x_in[t], 16))
            hi(0)
            act.dma_start(mem_in, mem[0].rearrange("(t p) d -> p t d", p=P)).then_inc(mem_in_s, 16)
            act.wait_ge(vec_ready, 1)
            act.wait_ge(c_one, 1)
            norm_hi("mix", 0)
            act.dma_start(wr[:, :, :], w_router[0].rearrange("(k p) e -> p k e", p=P)).then_inc(router_in, 16)
            hi(1)
            for n, (kind, L, j) in enumerate(units):
                if n < NA - 1 and (kind, j) != ("cout", 1):
                    hi(n + 2)
                if (kind, L, j) == ("a", 0, 0):
                    squares(norm_id("mem", 0), mem_in, BY_TILE, lambda i, t: (mem_in_s, 16))
                if (kind, L, j) == ("a", 0, 1):
                    for b in range(4):
                        copy_hi(memT[:, 2 * b:2 * b + 2, :],
                                bk(("norm", 1, b))[:, :].rearrange("p (c s) -> p c s", c=2),
                                ("norm", 1, b), ht_hi)
                if kind == "b":
                    if L or j:
                        act.wait_ge(cu_ready, 2 * L + j)
                    act.wait_ge(*full(("b", L, j)))
                    a.activation(sg, bk(("b", L, j))[:, :].rearrange("p (c s) -> p c s", c=2),
                                 ACT.Sigmoid).then_inc(sig_b, 1)
                if kind == "pin":
                    act.wait_ge(*full(("pin", L, j)))
                    if L:
                        act.wait_ge(s_lo, CC * L)
                    a.activation(pu[:, 2 * j:2 * j + 2, PPAD:PPAD + S],
                                 bk(("pin", L, j))[:, :].rearrange("p (c s) -> p c s", c=2),
                                 ACT.Copy).then_inc(pu_ready, 1)
                if kind == "gate":
                    act.wait_ge(*full(("gate", L, j)))
                    a.activation(gates[:, 2 * j:2 * j + 2, :],
                                 bk(("gate", L, j))[:, :].rearrange("p (c s) -> p c s", c=2),
                                 ACT.Sigmoid).then_inc(gate_ready, 1)
                if (kind, L, j) in (("b", 0, 1), ("gu", 0, 5)):
                    ML = 0 if kind == "b" else 1
                    act.wait_ge(ht_hi, 4 * norm_id("mem", 0) + 4)
                    for c in range(KC):
                        a.activation(mTh[:, c, :], memT[:, c, :], ACT.Copy,
                                     scale=gcol("mem", ML, c)).then_inc(mT_hi, 1)
                if kind == "gate" and j == 5:
                    act.wait_ge(pool_step, POOL_STEPS * (L + 1))
                    a.activation(SH[:, 0:4:2, :], s1[:, 0:4:2, PPAD:PPAD + S], ACT.Copy).then_inc(pooled_hi, 1)
                    a.activation(SH[:, 1:4:2, :], s2[:, 0:3:2, PPAD:PPAD + S], ACT.Copy).then_inc(pooled_hi, 1)
                if kind == "k":
                    act.wait_ge(*full(("k", L, j)))
                    a.activation(kT[:, 2 * j:2 * j + 2, :],
                                 bk(("k", L, j))[:, :].rearrange("p (c s) -> p c s", c=2),
                                 ACT.Copy).then_inc(kT_ready, 1)
                if (kind, j) == ("v", 0):
                    act.wait_ge(cen_ready, L + 1)
                    a.activation(sqc, acc, ACT.Square).then_inc(csq_ready, 1)
                    a.activation(unused[:, 2 * L:2 * L + 1], ones[:, 0:1], ACT.Sqrt)
                if kind == "v" and j == 1:
                    act.wait_ge(cvar, L + 1)
                    a.activation(sqc[:, 0, :], sqc[:, 1, :], ACT.Sqrt).then_inc(cstd, 1)
                    a.activation(unused[:, 2 * L + 1:2 * L + 2], ones[:, 0:1], ACT.Silu)
                    v_copies(L, 0)
                    for c in range(CC):
                        act.wait_ge(cnorm, CC * L + c + 1)
                        a.activation(sgc[:, c, :], acc[:, c, :], ACT.Silu, bias=col(LB0, L, CC, c),
                                     scale=col(LG0, L, CC, c)).then_inc(csilu, 1)
                        if c:
                            act.wait_ge(csilu, CC * L + c)
                            a.activation(SH[:, c - 1, :], sgc[:, c - 1, :], ACT.Copy).then_inc(s_hi, 1)
                    act.wait_ge(csilu, CC * L + CC)
                    a.activation(SH[:, CC - 1, :], sgc[:, CC - 1, :], ACT.Copy).then_inc(s_hi, 1)
                if kind == "cout":
                    for b in (2 * j, 2 * j + 1):
                        if b == 1:
                            hi(n + 3)
                        act.wait_ge(z_ready, 4 * L + b + 1)
                        a.activation(XH[:, 2 * b:2 * b + 2, :], gates[:, 8 + 2 * b:10 + 2 * b, :],
                                     ACT.Copy).then_inc(z_hi, 1)
                if (kind, j) in (("mix", 2), ("q", 0)):
                    norm_hi("xattn", L, (0, 1) if kind == "mix" else (2, 3))
                    x_squares("xattn", L, "mix", kind == "q")
                if (kind, j) == ("xo", 2):
                    norm_hi("ffn", L, (0, 1))
                    x_squares("ffn", L, "xo", 0)
                if (kind, L, j) in (("xo", 1, 3), ("gu", 0, 0)):
                    norm_hi("ffn", L, (2, 3))
                    x_squares("ffn", L, "xo", 1)
                if kind == "q":
                    act.wait_ge(*full(("q", L, j)))
                    a.activation(qT[:, 2 * j:2 * j + 2, :],
                                 bk(("q", L, j))[:, :].rearrange("p (c s) -> p c s", c=2),
                                 ACT.Copy).then_inc(qT_ready, 1)
                if (kind, j) == ("q", 3):
                    act.wait_ge(rq_ready, L + 1)
                    for b in range(4):
                        act.wait_ge(nmx_ready, 4 * L + b + 1)
                        for h in range(2):
                            i = 2 * b + h
                            a.activation(prob[:, i, :], bk(("score", L, b))[:, h * S:h * S + S], ACT.Exp,
                                         bias=smx[:, 1, i:i + 1], scale=rq[:, b // 2:b // 2 + 1],
                                         accum_out=smx[:, 2, i:i + 1]).then_inc(p_exp, 1)
                if (kind, L, j) == ("xo", 1, 0):
                    act.dma_start(gain_rows, g_ffn[1:2, :].to_broadcast([P, D])).then_inc(grow_in, 16)
                    act.wait_ge(router_in, 16)
                    a.activation(wrh[:, :, :], wr[:, :, :], ACT.Copy).then_inc(wr_hi, 1)
                if (kind, j) == ("v", 3):
                    v_copies(L, 1)
                    for h in range(NH):
                        act.wait_ge(*full(("pT", L, h)))
                        a.activation(pT[:, 2 * h:2 * h + 2, :],
                                     bk(("pT", L, h))[:, :].rearrange("p (c s) -> p c s", c=2),
                                     ACT.Copy).then_inc(pT_ready, 1)
                    for h in range(NH):
                        act.wait_ge(*full(("pv", L, h)))
                        a.activation(XH[:, 2 * h:2 * h + 2, :],
                                     bk(("pv", L, h))[:, :].rearrange("p (c s) -> p c s", c=2),
                                     ACT.Copy).then_inc(o_hi, 1)
                if (kind, L, j) == ("xo", 1, 3):
                    act.wait_ge(*full(("logitsT",)))
                    a.activation(lgT[:, :], bk(("logitsT",))[0:NE, 0:S], ACT.Copy).then_inc(lgT_ready, 1)

                    def xn_hi(t):
                        act.wait_ge(xn_ready, 2 * XN["ffn", 1] + t + 1)
                        a.activation(xnh[:, t], xn[:, t], ACT.Copy).then_inc(xnh_ready, 1)
                    xn_hi(0)
                    hi(NA + 1)
                    act.wait_ge(route, ROUTE_DIFF)
                    a.activation(m12[:, 3, :], m12[:, 2, :], ACT.Exp).then_inc(ex_ready, 1)
                    act.wait_ge(zero_ready, 1)
                    a.activation(cnts[:, 3:4], cnts[:, 2:3], ACT.Silu).then_inc(tab_ready, 1)
                    xn_hi(1)
                if kind == "gu" and j % 2 == 1:
                    act.wait_ge(rstd_ready, norm_id("ffn", 0) + 1)
                    for t in range(NT):
                        act.wait_ge(*full(("gu", L, j // 2, t)))
                        if j > 1:
                            act.wait_ge(h_ready, 2 * (j // 2))
                        a.activation(sg[:, t, :], bk(("gu", L, j // 2, t))[:, 0:FB], ACT.Silu,
                                     scale=rs[:, norm_id("ffn", 0), t:t + 1]).then_inc(silu_done, 1)
                    if j == 1:
                        act.wait_ge(*full(("hT", L, 0)))
                        a.activation(hTh[:, :, :], bk(("hT", L, 0))[:, :].rearrange("p (c s) -> p c s", c=2),
                                     ACT.Copy).then_inc(hT_hi, 1)
                if kind == "down" and j < NB - 1:
                    act.wait_ge(*full(("hT", L, j + 1)))
                    a.activation(hTh[:, :, :], bk(("hT", L, j + 1))[:, :].rearrange("p (c s) -> p c s", c=2),
                                 ACT.Copy).then_inc(hT_hi, 1)
                if kind == "down" and j == NB - 1:
                    squares(norm_id("mix", 1), xs, BY_TILE,
                            lambda i, t: (x_add, xadd(0, "ffn", 2 * t + i % 2)))
                    norm_hi("mix", 1)


            def gather_hi(banks, at_full):
                for b in banks:
                    act.wait_ge(*at_full(b))
                    a.activation(XH[:, 2 * b:2 * b + 2, 0:P], gathered(b), ACT.Copy).then_inc(g_hi, 1)
            gather_hi(range(4), lambda b: full(("gather", b)))
            act.wait_ge(nit_ready, 1)
            n = act.value_load(n_it[0:1, 0:1], min_val=NE, max_val=2 * NE)
            with act.Fori(0, n) as it:
                act.wait_ge(tab_ready, it + 1)
                a.activation(cnts[:, 3:4], cnts[:, 2:3], ACT.Silu).then_inc(tab_ready, 1)

                def hi_m(i):
                    s = (i % NM) % RING_M
                    extra = per_slot[s] if i >= NM else 0
                    act.wait_ge(raw_landed[s], it * per_slot[s] + (landed_base[s] + extra + moe_landed[i % NM]))
                    act.wait_ge(*mthrough(i - HL, it))
                    a.activation(WH[:, (NA + i) % HL, :], raw[s], ACT.Copy).then_inc(hi_ready, 1)

                def hT_hi_m(b):
                    act.wait_ge(*mfull(("hT", b), it))
                    a.activation(hTh[:, 0, :], bank[2][:, 0:2 * P], ACT.Copy).then_inc(hT_hi, 1)

                for i, (kind, j) in enumerate(moe):
                    hi_m(i + 2)
                    b = j // 2
                    if kind == "gu" and j % 2 == 0 and b >= 1:
                        hT_hi_m(b - 1)
                    if kind == "gu" and j == 3:
                        act.wait_ge(*mfull(("PT",), it))
                        a.activation(PT, bank[7][:, 0:S], ACT.Copy).then_inc(PT_ready, 1)
                    if kind == "gu" and j % 2 == 1:
                        act.wait_ge(*mfull(("gu", b), it))
                        act.wait_ge(h_ready, it * NB + (2 * NB + b))
                        a.activation(sg[:, 0, :], bank[b % 2][:, 0:FB], ACT.Silu).then_inc(silu_done, 1)
                    if kind == "gu" and j == 2 * 8 + 1:
                        act.wait_ge(PM_ready, it + 2)
                        a.activation(PMr, PM, ACT.Copy).then_inc(PMr_ready, 1)
                    if kind == "down" and j == NB - 2:
                        hT_hi_m(NB - 1)
                        gather_hi((0, 1), lambda b: mfull(("gather", b), it))
                    if kind == "down" and j == NB - 1:
                        for m in range(2):
                            act.wait_ge(*mfull(("y", m), it))
                            a.activation(yh[:, m, :], bank[3 + m][:, :], ACT.Copy).then_inc(y_hi, 1)
                        gather_hi((2, 3), lambda b: mfull(("gather", b), it))

            act.wait_ge(h_ready, n * NB + 2 * NB)
            act.wait_ge(PM_ready, n + 1)
            act.dma_start(gain_rows, g_final.rearrange("(o d) -> o d", o=1).to_broadcast([P, D])
                          ).then_inc(gfin_in, 16)
            squares(norm_id("final", 0), xs, BY_HALF, lambda i, t: (x_add, n * 4 + xadd(1, "ffn", i - 4)))

        @block.vector
        def _(dve):
            v = nc.vector
            dve.wait_ge(c_cnt0, 1 + CC)
            v.reciprocal(icnt[:, :, :], m16[:, :, :]).then_inc(c_cnt, 1)
            def lo(n):
                dve.wait_ge(hi_ready, n + 1)
                s = raw[n % RING_A] if n < NA else raw[(n - NA) % RING_M]
                w = width(n)
                v.tensor_tensor(WL[:, n % HL, 0:w], s[:, 0:w], WH[:, n % HL, 0:w].bitcast(F32),
                                ALU.subtract).then_inc(lo_ready, 1)

            def norm_var(N):
                dve.wait_ge(sq_done, 4 * N + 4)
                v.scalar_tensor_tensor(vv[:, N, :], ss[:, N, :, 0], EPS, ss[:, N, :, 1], ALU.add,
                                       ALU.add).then_inc(var_ready, 1)

            def norm_scale(N, src):
                norm_var(N)
                dve.wait_ge(rstd_ready, N + 1)
                for t in range(NT):
                    v.tensor_scalar(xn[:, t], src[:, t], rs[:, N, t:t + 1], None, ALU.mult).then_inc(xn_ready, 1)

            def norm_lo(kind, L, pieces=range(4)):
                N = norm_id(kind, L)
                for b in pieces:
                    dve.wait_ge(ht_hi, 4 * N + b + 1)
                    ps = bk(("norm", N, b))[:, :].rearrange("p (c s) -> p c s", c=2)
                    for c in range(2):
                        k = 2 * b + c
                        ins = v.scalar_tensor_tensor(XL[:, k, :], ps[:, c, :], gcol(kind, L, k),
                                                     XH[:, k, :].bitcast(F32), ALU.mult, ALU.subtract)
                    ins.then_inc(ht_lo, 1)

            conv_n = [0]

            def conv_taps(L, count):
                for _ in range(count):
                    i = conv_n[0] - L * TAPS * CC
                    if i >= TAPS * CC:
                        return
                    half, i = divmod(i, 2 * TAPS)
                    k, c = divmod(i, 2)
                    c += 2 * half
                    if k == 0:
                        if c % 2 == 0:
                            dve.wait_ge(cu_ready, 2 * L + half + 1)
                        v.tensor_scalar(acc[:, c, :], cu[:, c, 0:S], tap(L, 0, c), col(BD0, L, CC, c),
                                        ALU.mult, ALU.add).then_inc(conv_step, 1)
                    else:
                        dve.wait_ge(conv_step, conv_n[0] - 1)
                        v.scalar_tensor_tensor(acc[:, c, :], cu[:, c, k:k + S], tap(L, k, c), acc[:, c, :],
                                               ALU.mult, ALU.add).then_inc(conv_step, 1)
                    conv_n[0] += 1

            def add_x(L, stage, kind, halves):
                for m in halves:
                    for t in range(NT):
                        label = (kind, L, m, t)
                        dve.wait_ge(*full(label))
                        v.tensor_tensor(xs[:, t, m * 512:m * 512 + 512], xs[:, t, m * 512:m * 512 + 512],
                                        bk(label)[:, :], ALU.add).then_inc(x_add, 1)

            norm_scale(norm_id("mix", 0), xs)
            lo(0)
            dve.wait_ge(*full(("vec",)))
            v.tensor_copy(vec[:, 0:VROWS], bank[0][:, 0:VROWS]).then_inc(c_cnt, 1)
            v.tensor_copy(bias[:, :], bank[0][:, 504:504 + NE]).then_inc(c_cnt, 1)
            v.tensor_copy(vec[:, VROWS:], bank[0][:, P:P + DEPTH * TAPS * CC]).then_inc(vec_ready, 1)
            dve.wait_ge(vec_ready, 1)
            dve.wait_ge(c_cnt, 3)
            norm_lo("mix", 0)
            lo(1)
            for n, (kind, L, j) in enumerate(units):
                if n < NA - 1 and (kind, j) not in (("cout", 1), ("q", 0)):
                    lo(n + 2)
                if (kind, L, j) == ("a", 0, 0):
                    norm_scale(norm_id("mem", 0), mem_in)
                    dve.sem_inc(ht_lo, 4)
                if kind == "b":
                    dve.wait_ge(sig_b, 2 * L + j + 1)
                    dve.wait_ge(*full(("a", L, j)))
                    dve.wait_ge(c_pad, 2)
                    v.tensor_tensor(cu[:, 2 * j:2 * j + 2, PAD:PAD + S],
                                    bk(("a", L, j))[:, :].rearrange("p (c s) -> p c s", c=2), sg,
                                    ALU.mult).then_inc(cu_ready, 1)
                    conv_taps(L, 5)
                if (kind, j) == ("a", 1):
                    conv_taps(L, 7)
                if kind == "pin":
                    conv_taps(L, 4 if (L, j) == (0, 0) else 8)
                if kind == "gate":
                    conv_taps(L, 8)
                if (kind, L, j) in (("pin", 0, 0), ("gu", 0, 5)):
                    ML = 0 if kind == "pin" else 1
                    for c in range(KC):
                        dve.wait_ge(mT_hi, 8 * ML + c + 1)
                        v.scalar_tensor_tensor(mTl[:, c, :], memT[:, c, :], gcol("mem", ML, c),
                                               mTh[:, c, :].bitcast(F32), ALU.mult,
                                               ALU.subtract).then_inc(mT_lo, 1)
                if kind == "gate" and j == 5:
                    dve.wait_ge(pooled_hi, 2 * L + 1)
                    v.tensor_tensor(SL[:, 0:4:2, :], s1[:, 0:4:2, PPAD:PPAD + S],
                                    SH[:, 0:4:2, :].bitcast(F32), ALU.subtract).then_inc(pooled_lo, 1)
                    dve.wait_ge(pooled_hi, 2 * L + 2)
                    v.tensor_tensor(SL[:, 1:4:2, :], s2[:, 0:3:2, PPAD:PPAD + S],
                                    SH[:, 1:4:2, :].bitcast(F32), ALU.subtract).then_inc(pooled_lo, 1)
                if kind == "wpool":
                    for b in range(4):
                        dve.wait_ge(*full(("wpool", L, b)))
                        for c in range(2):
                            k = 2 * b + c
                            v.scalar_tensor_tensor(gates[:, k, :], bk(("wpool", L, b))[:, c * S:c * S + S],
                                                   col(PS0, L, KC, k), gates[:, k, :], ALU.mult,
                                                   ALU.mult).then_inc(zp_ready, 1)
                if kind == "k":
                    conv_taps(L, TAPS * CC if j == 3 else 8)
                if (kind, j) == ("v", 0):
                    dve.wait_ge(*full(("mean", L)))
                    v.scalar_tensor_tensor(acc, bank[4][:, 0:S].unsqueeze(1).to_broadcast([P, CC, S]),
                                           -1.0 / CW, acc, ALU.mult, ALU.add).then_inc(cen_ready, 1)
                if (kind, j) == ("v", 1):
                    dve.wait_ge(*full(("var", L)))
                    v.tensor_scalar(sqc[:, 1, :], bank[5][:, 0:S], 1.0 / CW, EPS, ALU.mult, ALU.add).then_inc(cvar, 1)
                    dve.wait_ge(cstd, L + 1)
                    v.reciprocal(sqc[:, 2, :], sqc[:, 0, :]).then_inc(crstd, 1)
                    dve.wait_ge(crstd, L + 1)
                    for c in range(CC):
                        v.tensor_tensor(acc[:, c, :], acc[:, c, :], sqc[:, 2, :], ALU.mult).then_inc(cnorm, 1)
                    for c in range(CC):
                        dve.wait_ge(s_hi, CC * L + c + 1)
                        v.tensor_tensor(SL[:, c, :], sgc[:, c, :], SH[:, c, :].bitcast(F32),
                                        ALU.subtract).then_inc(s_lo, 1)
                if kind == "cout":
                    for b in (2 * j, 2 * j + 1):
                        label = ("cout", L, b)
                        dve.wait_ge(*full(label))
                        gc = gates[:, 8 + 2 * b:10 + 2 * b, :]
                        v.tensor_tensor(gc, bk(label)[:, :].rearrange("p (c s) -> p c s", c=2), gc,
                                        ALU.mult).then_inc(zc_ready, 1)
                        dve.wait_ge(zc_ready, 4 * L + b + 1)
                        v.tensor_tensor(gc, gc, gates[:, 2 * b:2 * b + 2, :], ALU.add).then_inc(z_ready, 1)
                        dve.wait_ge(z_hi, 4 * L + b + 1)
                        v.tensor_tensor(XL[:, 2 * b:2 * b + 2, :], gc, XH[:, 2 * b:2 * b + 2, :].bitcast(F32),
                                        ALU.subtract).then_inc(z_lo, 1)
                        if b == 1:
                            lo(n + 3)
                if kind == "mix" and j % 2:
                    add_x(L, "mix", "mix", (j // 2,))
                if (kind, j) == ("mix", 2):
                    norm_lo("xattn", L, (0, 1))
                if (kind, j) == ("q", 0):
                    norm_lo("xattn", L, (2, 3))
                    lo(n + 2)
                if (kind, j) == ("q", 1):
                    N = norm_id("xattn", L)
                    norm_var(N)
                    dve.wait_ge(rstd_ready, N + 1)
                    v.tensor_scalar(rq[:, :], rs[:, N, :], HD ** -0.5, None, ALU.mult).then_inc(rq_ready, 1)
                if (kind, j) == ("q", 3):
                    dve.wait_ge(rq_ready, L + 1)
                    for b in range(4):
                        dve.wait_ge(*full(("score", L, b)))
                        if L:
                            dve.wait_ge(p_norm, 8 * L)
                        v.tensor_reduce(smx[:, 0, 2 * b:2 * b + 2],
                                        bk(("score", L, b))[:, :].rearrange("p (c s) -> p c s", c=2),
                                        X_AXIS, ALU.max).then_inc(mx_ready, 1)
                        dve.wait_ge(mx_ready, 4 * L + b + 1)
                        v.tensor_scalar(smx[:, 1, 2 * b:2 * b + 2], smx[:, 0, 2 * b:2 * b + 2],
                                        rq[:, b // 2:b // 2 + 1], -1.0, ALU.mult, ALU.mult).then_inc(nmx_ready, 1)
                    for b in range(4):
                        dve.wait_ge(p_exp, 8 * L + 2 * b + 2)
                        v.reciprocal(smx[:, 2, 2 * b:2 * b + 2], smx[:, 2, 2 * b:2 * b + 2]).then_inc(rden, 1)
                        dve.wait_ge(rden, 4 * L + b + 1)
                        for i in (2 * b, 2 * b + 1):
                            v.tensor_scalar(prob[:, i, :], prob[:, i, :], smx[:, 2, i:i + 1], None,
                                            ALU.mult).then_inc(p_norm, 1)
                if (kind, j) == ("v", 3):
                    for h in range(NH):
                        dve.wait_ge(o_hi, 4 * L + h + 1)
                        v.tensor_tensor(XL[:, 2 * h:2 * h + 2, :],
                                        bk(("pv", L, h))[:, :].rearrange("p (c s) -> p c s", c=2),
                                        XH[:, 2 * h:2 * h + 2, :].bitcast(F32), ALU.subtract).then_inc(o_lo, 1)
                if kind == "xo" and j % 2:
                    add_x(L, "xo", "xo", (j // 2,))
                if (kind, j) == ("xo", 2):
                    norm_lo("ffn", L, (0, 1))
                if (kind, L, j) == ("xo", 1, 2):
                    dve.wait_ge(wr_hi, 1)
                    dve.wait_ge(c_iota, 1)
                    for t in range(NT):
                        v.tensor_scalar(PRI[:, t, :], iota[:, 0:NE], -1.0, float(NE + 1), ALU.mult,
                                        ALU.add).then_inc(sel_ready, 1)
                    v.memset(cnts[:, 2:3], 0.0).then_inc(zero_ready, 1)
                    v.tensor_tensor(wrl[:, :, :], wr[:, :, :], wrh[:, :, :].bitcast(F32),
                                    ALU.subtract).then_inc(wr_lo, 1)
                if (kind, L, j) in (("xo", 1, 3), ("gu", 0, 0)):
                    norm_lo("ffn", L, (2, 3))
                    norm_var(norm_id("ffn", L))
                if (kind, L, j) == ("xo", 1, 3):
                    N = norm_id("ffn", 1)
                    dve.wait_ge(rstd_ready, N + 1)
                    dve.wait_ge(grow_in, 16)

                    def xn_with_gain(t):
                        v.scalar_tensor_tensor(xn[:, t, :], xs[:, t, :], rs[:, N, t:t + 1], gain_rows, ALU.mult,
                                               ALU.mult).then_inc(xn_ready, 1)
                    xn_with_gain(0)
                if kind == "gu" and j % 2 == 1:
                    b = j // 2
                    for t in range(NT):
                        dve.wait_ge(silu_done, 2 * b + t + 1)
                        if b:
                            dve.wait_ge(hT_hi, b)
                        v.scalar_tensor_tensor(hh[:, t, :], bank[t][:, FB:2 * FB],
                                               rs[:, norm_id("ffn", 0), t:t + 1], sg[:, t, :], ALU.mult,
                                               ALU.mult).then_inc(h_ready, 1)
                    if j == 1:
                        dve.wait_ge(hT_hi, 1)
                        v.tensor_tensor(hTl[:, :, :], bank[2][:, :].rearrange("p (c s) -> p c s", c=2),
                                        hTh[:, :, :].bitcast(F32), ALU.subtract).then_inc(hT_lo, 1)
                if kind == "down" and j < NB - 1:
                    dve.wait_ge(hT_hi, j + 2)
                    v.tensor_tensor(hTl[:, :, :], bank[2][:, :].rearrange("p (c s) -> p c s", c=2),
                                    hTh[:, :, :].bitcast(F32), ALU.subtract).then_inc(hT_lo, 1)
                if kind == "down" and j == NB - 1:
                    for t in range(NT):
                        for m in range(2):
                            label = ("ffn", L, m, t)
                            dve.wait_ge(*full(label))
                            xv = xs[:, t, m * 512:m * 512 + 512]
                            v.tensor_tensor(xv, xv, bk(label)[:, :], ALU.add).then_inc(x_add, 1)
                    norm_scale(norm_id("mix", 1), xs)
                    norm_lo("mix", 1)

            rt = [0]

            def link(ins):
                rt[0] += 1
                ins.then_inc(route, 1)
                dve.wait_ge(route, rt[0])

            def wide(c):
                return m12[:, c, :].unsqueeze(2).to_broadcast([P, NT, NE])

            dve.wait_ge(*full(("logits",)))
            for t in range(NT):
                v.scalar_tensor_tensor(LOG[:, t, :], bk(("logits",))[:, t * NE:t * NE + NE],
                                       rs[:, norm_id("ffn", 1), t:t + 1], bias[:, :], ALU.mult,
                                       ALU.add).then_inc(sel_ready, 1)
            dve.wait_ge(sel_ready, 4)

            def priorities(src, m):
                for t in range(NT):
                    v.scalar_tensor_tensor(SC[:, t, :], src[:, t, :], m12[:, m, t:t + 1], PRI[:, t, :],
                                           ALU.is_equal, ALU.mult).then_inc(route, 1)
                rt[0] += NT

            link(v.tensor_reduce(m12[:, 0, :], LOG, X_AXIS, ALU.max))
            priorities(LOG, 0)
            dve.wait_ge(route, rt[0])
            link(v.tensor_reduce(m12[:, 4, :], SC, X_AXIS, ALU.max))
            link(v.tensor_tensor(F1, SC, wide(4), ALU.is_equal))
            link(v.scalar_tensor_tensor(L2, F1, -3.0e38, LOG, ALU.mult, ALU.add))
            link(v.tensor_reduce(m12[:, 1, :], L2, X_AXIS, ALU.max))
            priorities(L2, 1)
            v.tensor_tensor(m12[:, 2, :], m12[:, 1, :], m12[:, 0, :], ALU.subtract).then_inc(route, 1)
            dve.wait_ge(route, rt[0])
            rt[0] += 1
            assert rt[0] == ROUTE_DIFF
            link(v.tensor_reduce(m12[:, 5, :], SC, X_AXIS, ALU.max))
            link(v.tensor_tensor(F2, SC, wide(5), ALU.is_equal))
            v.tensor_tensor(SEL, F1, F2, ALU.add).then_inc(sel_ready, 1)
            xn_with_gain(1)
            dve.wait_ge(*full(("rank",)))
            link(v.scalar_tensor_tensor(slotT[:, :, 0:NE],
                                        bk(("rank",))[:, 0:NT * NE].rearrange("p (t e) -> p t e", t=NT), 1.0,
                                        SEL, ALU.add, ALU.mult))
            assert rt[0] == ROUTE_RANK
            for t in range(NT):
                ins = v.tensor_scalar(PMr[:, t, :], iota[:, :], slotT[:, t, 0:1], None, ALU.is_equal)
            ins.then_inc(PMr_ready, 1)
            for t in range(NT):
                ins = v.tensor_scalar(PM[:, t, :], iota[:, :], slotT[:, t, 0:1], None, ALU.is_equal)
            ins.then_inc(PM_ready, 1)
            for t in range(NT):
                dve.wait_ge(xnh_ready, t + 1)
                v.tensor_tensor(xnl[:, t], xn[:, t], xnh[:, t].bitcast(F32),
                                ALU.subtract).then_inc(xnl_ready, 1)
            link(v.tensor_scalar(slotT[:, :, NE:2 * NE], slotT[:, :, 0:NE], -float(P), None, ALU.add))
            link(v.memset(slotT[:, :, 2 * NE:2 * NE + 1], 0.0))
            dve.wait_ge(*full(("count",)))
            link(v.tensor_reduce(cnts[:, 0:1], bk(("count",))[:, 0:NE], X_AXIS, ALU.max))
            assert rt[0] == ROUTE_COUNT
            link(v.tensor_scalar(cnts[:, 1:2], cnts[:, 0:1], float(P), float(NE), ALU.is_gt, ALU.mult))
            v.tensor_scalar(n_it[:, :], cnts[0:1, 1:2], float(NE), None, ALU.add).then_inc(nit_ready, 1)
            lo(NA + 1)

            def select():
                for t in range(NT):
                    ins = v.tensor_scalar(PM[:, t, :], iota[:, :], cur[:, 0, t:t + 1], None, ALU.is_equal)
                ins.then_inc(PM_ready, 1)

            def gather_lo(banks, want):
                for b in banks:
                    dve.wait_ge(g_hi, want(b))
                    v.tensor_tensor(XL[:, 2 * b:2 * b + 2, 0:P], gathered(b),
                                    XH[:, 2 * b:2 * b + 2, 0:P].bitcast(F32), ALU.subtract).then_inc(g_lo, 1)
            gather_lo(range(4), lambda b: b + 1)
            dve.wait_ge(ex_ready, 1)
            link(v.tensor_scalar(m12[:, 6, :], m12[:, 3, :], 1.0, None, ALU.add))
            link(v.reciprocal(m12[:, 6, :], m12[:, 6, :]))
            link(v.tensor_tensor(m12[:, 7, :], m12[:, 3, :], m12[:, 6, :], ALU.mult))
            link(v.tensor_tensor(COM, F1, wide(6), ALU.mult))
            link(v.tensor_tensor(TMP, F2, wide(7), ALU.mult))
            for c in range(2):
                v.tensor_tensor(combT[:, :, c * NE:c * NE + NE], COM, TMP, ALU.add).then_inc(route, 1)
            dve.wait_ge(route, rt[0] + 2)
            dve.sem_inc(y_lo, 2)
            dve.wait_ge(nit_ready, 1)
            n = dve.value_load(n_it[0:1, 0:1], min_val=NE, max_val=2 * NE)
            with dve.Fori(0, n) as it:
                def lo_m(i):
                    dve.wait_ge(hi_ready, it * NM + (NA + i + 1))
                    v.tensor_tensor(WL[:, (NA + i) % HL, :], raw[(i % NM) % RING_M],
                                    WH[:, (NA + i) % HL, :].bitcast(F32), ALU.subtract).then_inc(lo_ready, 1)

                def hT_lo_m(b):
                    dve.wait_ge(hT_hi, it * NB + (NB + b + 1))
                    v.tensor_tensor(hTl[:, 0, :], bank[2][:, 0:2 * P], hTh[:, 0, :].bitcast(F32),
                                    ALU.subtract).then_inc(hT_lo, 1)

                for i, (kind, j) in enumerate(moe):
                    lo_m(i + 2)
                    b = j // 2
                    if kind == "gu" and j % 2 == 0 and b >= 1:
                        hT_lo_m(b - 1)
                    if kind == "gu" and j % 2 == 1:
                        dve.wait_ge(silu_done, it * NB + (2 * NB + b + 1))
                        v.tensor_tensor(hh[:, 0, :], sg[:, 0, :], bank[b % 2][:, FB:2 * FB],
                                        ALU.mult).then_inc(h_ready, 1)
                    if kind == "gu" and j == 2 * 4 + 1:
                        v.tensor_copy(cur[:, 0, :], slotT[:, :, bass.ds(it + 1, 1)].rearrange("p t o -> p (t o)")
                                      ).then_inc(cur_ready, 1)
                        v.tensor_copy(cur[:, 1, :], combT[:, :, bass.ds(it, 1)].rearrange("p t o -> p (t o)")
                                      ).then_inc(cur_ready, 1)
                    if kind == "gu" and j == 2 * 7 + 1:
                        dve.wait_ge(cur_ready, it * 2 + 2)
                        dve.wait_ge(PT_ready, it + 1)
                        select()
                    if kind == "down" and j == NB - 2:
                        hT_lo_m(NB - 1)
                        gather_lo((0, 1), lambda b: it * 4 + (4 + b + 1))
                    if kind == "down" and j == NB - 1:
                        for m in range(2):
                            dve.wait_ge(y_hi, it * 2 + (m + 1))
                            v.tensor_tensor(yl[:, m, :], bank[3 + m][:, :], yh[:, m, :].bitcast(F32),
                                            ALU.subtract).then_inc(y_lo, 1)
                        gather_lo((2, 3), lambda b: it * 4 + (4 + b + 1))
                        for r in range(4):
                            m, t = divmod(r, 2)
                            dve.wait_ge(*mfull(("scatter", r), it))
                            xv = xs[:, t, m * 512:m * 512 + 512]
                            v.scalar_tensor_tensor(xv, bank[SC_BANK[r]][:, :], cur[:, 1, t:t + 1], xv,
                                                   ALU.mult, ALU.add).then_inc(x_add, 1)

            N = norm_id("final", 0)
            norm_var(N)
            dve.wait_ge(rstd_ready, N + 1)
            dve.wait_ge(gfin_in, 16)
            for t in range(NT):
                v.scalar_tensor_tensor(xn[:, t, :], xs[:, t, :], rs[:, N, t:t + 1], gain_rows, ALU.mult,
                                       ALU.mult).then_inc(out_ready, 1)

        @block.tensor
        def _(pe):
            te = nc.tensor

            def claim(label):
                if plan.before[label]:
                    pe.wait_ge(*read(plan.before[label]))
                return bank[plan.of[label][0]]

            def done(ins, label):
                ins.then_inc(bank_full[plan.of[label][0]], 1)

            def mm3(out, ah, al, bh, bl, start, stop):
                te.matmul(out, ah, bh, start=start, stop=False)
                te.matmul(out, ah, bl, start=False, stop=False)
                return te.matmul(out, al, bh, start=False, stop=stop)

            def split(n):
                pe.wait_ge(lo_ready, n + 1)
                return WH[:, n % HL, :], WL[:, n % HL, :]

            def to_feature_major(kind, L, src, ready, pieces=range(4)):
                for b in pieces:
                    label = ("norm", norm_id(kind, L), b)
                    ps = claim(label)
                    for c in range(2):
                        for t in range(NT):
                            pe.wait_ge(*ready(t))
                            k = 2 * b + c
                            ins = te.transpose(ps[:, c * S + t * P:c * S + t * P + P],
                                               src[:, t, k * P:k * P + P], ident[:, :])
                    done(ins, label)

            def norm_T(kind, L):
                to_feature_major(kind, L, xn, lambda t: (xn_ready, 2 * XN[kind, L] + t + 1))

            def x_T(kind, L, stage, m):
                N, pieces = norm_id(kind, L), (2 * m, 2 * m + 1)
                ps = {b: claim(("norm", N, b)) for b in pieces}
                for t in range(NT):
                    pe.wait_ge(x_add, xadd(L, stage, 2 * m + t))
                    for b in pieces:
                        for c in range(2):
                            k = 2 * b + c
                            ins = te.transpose(ps[b][:, c * S + t * P:c * S + t * P + P],
                                               xs[:, t, k * P:k * P + P], ident[:, :])
                        if t == NT - 1:
                            done(ins, ("norm", N, b))

            pe.wait_ge(c_id, 2)
            pe.wait_ge(c_one, 1)
            norm_T("mix", 0)
            pe.wait_ge(rows_in, 16 * (8 + 1 + 1))
            ps = claim(("vec",))
            te.transpose(ps[:, 0:VROWS], rows[0:VROWS, 0, :], ident[0:VROWS, 0:VROWS])
            R = TAPS * CC
            for L in range(DEPTH):
                te.transpose(ps[:, P + L * R:P + L * R + R], rows[0:R, 1 + L, :], ident[0:R, 0:R])
            done(te.matmul(ps[:, 504:504 + NE], ones[0:1, :], brow[0:1, :], start=True, stop=True), ("vec",))

            def feature_major(n, label, right_h, right_l, k_chunks, cols, ready=None):
                wh, wl = split(n)
                wh = wh.rearrange("p (k n) -> p k n", k=k_chunks)
                wl = wl.rearrange("p (k n) -> p k n", k=k_chunks)
                for ct in range(cols // P):
                    if ct % 2 == 0:
                        lab = label(ct // 2)
                        ps = claim(lab)
                    o = ps[:, (ct % 2) * S:(ct % 2) * S + S]
                    cs = slice(ct * P, ct * P + P)
                    for k in range(k_chunks):
                        if ready and ct == 0:
                            pe.wait_ge(*ready(k))
                        ins = mm3(o, wh[:, k, cs], wl[:, k, cs], right_h[:, k, :], right_l[:, k, :],
                                  k == 0, k == k_chunks - 1)
                    if ct % 2 == 1:
                        done(ins, lab)

            def q_part(L, j, c, chunks):
                wh, wl = split(index["q", L, j])
                wh = wh.rearrange("p (k n) -> p k n", k=KC)
                wl = wl.rearrange("p (k n) -> p k n", k=KC)
                ps = claim(("q", L, j)) if (c, chunks[0]) == (0, 0) else bk(("q", L, j))
                for k in chunks:
                    if (j, c) == (0, 0):
                        pe.wait_ge(ht_lo, 4 * norm_id("xattn", L) + k // 2 + 1)
                    ins = mm3(ps[:, c * S:c * S + S], wh[:, k, c * P:c * P + P], wl[:, k, c * P:c * P + P],
                              XH[:, k, :], XL[:, k, :], k == 0, k == KC - 1)
                if (c, chunks[-1]) == (1, KC - 1):
                    done(ins, ("q", L, j))

            def token_major(n, kind, L, j, left_h, left_l, ready=None):
                wh, wl = split(n)
                wh = wh.rearrange("p (k n) -> p k n", k=4)
                wl = wl.rearrange("p (k n) -> p k n", k=4)
                m, kh = divmod(j, 2)
                for t in range(NT):
                    label = (kind, L, m, t)
                    ps = claim(label) if kh == 0 else bk(label)
                    ts = slice(t * P, t * P + P)
                    for k in range(4):
                        kk = 4 * kh + k
                        if ready and t == 0:
                            pe.wait_ge(*ready(kk))
                        ins = mm3(ps[:, :], left_h[:, kk, ts], left_l[:, kk, ts], wh[:, k, :], wl[:, k, :],
                                  kk == 0, kk == KC - 1)
                    if kh == 1:
                        done(ins, label)
                if kh == 0:
                    ins.then_inc(unit_used, 1)

            for n, (kind, L, j) in enumerate(units):
                if kind in ("a", "b", "pin", "gate"):
                    feature_major(n, lambda i: (kind, L, j), XH, XL, KC, 256, (kind, j) == ("a", 0) and
                                  (lambda k: (ht_lo, 4 * norm_id("mix", L) + k // 2 + 1)))
                    if (kind, L, j) == ("b", 0, 0):
                        norm_T("mem", 0)
                elif kind == "wpool":
                    pe.wait_ge(pooled_lo, 2 * L + 2)
                    wh, wl = split(n)
                    for b in range(4):
                        ps = claim((kind, L, b))
                        for c in range(2):
                            cs = slice(b * 256 + c * P, b * 256 + c * P + P)
                            ins = mm3(ps[:, c * S:c * S + S], wh[:, cs], wl[:, cs], SH[:, b, :], SL[:, b, :],
                                      True, True)
                        done(ins, (kind, L, b))
                elif kind == "k":
                    if j == 0:
                        pe.wait_ge(mT_lo, 8 * L + 8)
                    feature_major(n, lambda i: (kind, L, j), mTh, mTl, KC, 256)
                elif kind == "cout":
                    feature_major(n, lambda i: (kind, L, 2 * j + i), SH, SL, CC, 512,
                                  lambda k: (s_lo, CC * L + k + 1))
                elif kind == "mix":
                    token_major(n, kind, L, j, XH, XL, j < 2 and (lambda k: (z_lo, 4 * L + k // 2 + 1)))
                    if j == 2:
                        x_T("xattn", L, "mix", 0)
                elif kind == "v":
                    token_major(n, kind, L, j, mTh, mTl)
                    if j == 0:
                        pe.wait_ge(conv_step, (L + 1) * TAPS * CC)
                        ps = claim(("mean", L))
                        for c in range(CC):
                            ins = te.matmul(ps[:, 0:S], ones[:, :], acc[:, c, :], start=(c == 0),
                                            stop=(c == CC - 1))
                        done(ins, ("mean", L))
                    if j == 1:
                        pe.wait_ge(csq_ready, L + 1)
                        ps = claim(("var", L))
                        for c in range(CC):
                            ins = te.matmul(ps[:, 0:S], ones[:, :], sqc[:, c, :], start=(c == 0),
                                            stop=(c == CC - 1))
                        done(ins, ("var", L))
                elif kind == "q":
                    if j == 0:
                        for i in range(2):
                            q_part(L, i, 0, (0, 1, 2, 3))
                        x_T("xattn", L, "mix", 1)
                        for i in range(2):
                            q_part(L, i, 0, (4, 5, 6, 7))
                            q_part(L, i, 1, range(KC))
                    elif j > 1:
                        for c in range(2):
                            q_part(L, j, c, range(KC))
                elif kind == "xo":
                    token_major(n, kind, L, j, XH, XL, j < 2 and (lambda k: (o_lo, 4 * L + k // 2 + 1)))
                    if j == 2:
                        x_T("ffn", L, "xo", 0)
                elif kind == "gu":
                    b = j // 2
                    wh, wl = split(n)
                    wh = wh.rearrange("p (k n) -> p k n", k=4)
                    wl = wl.rearrange("p (k n) -> p k n", k=4)
                    for t in range(NT):
                        label = ("gu", L, b, t)
                        ps = claim(label) if j % 2 == 0 else bk(label)
                        ts = slice(t * P, t * P + P)
                        for k in range(4):
                            kk = 4 * (j % 2) + k
                            if b == 0 and t == 0:
                                pe.wait_ge(ht_lo, 4 * norm_id("ffn", L) + kk // 2 + 1)
                            ins = mm3(ps[:, :], XH[:, kk, ts], XL[:, kk, ts], wh[:, k, :], wl[:, k, :],
                                      kk == 0, kk == KC - 1)
                        if j % 2:
                            done(ins, label)
                        if j == 0 and t == 0:
                            x_T("ffn", L, "xo", 1)
                    if j % 2 == 0:
                        ins.then_inc(unit_used, 1)
                elif kind == "down":
                    pe.wait_ge(hT_lo, j + 1)
                    wh, wl = split(n)
                    wh = wh.rearrange("p (k n) -> p k n", k=2)
                    wl = wl.rearrange("p (k n) -> p k n", k=2)
                    for t in range(NT):
                        for m in range(2):
                            label = ("ffn", L, m, t)
                            ps = claim(label) if j == 0 else bk(label)
                            for k in range(2):
                                ts = slice(t * P, t * P + P)
                                ms = slice(m * 512, m * 512 + 512)
                                ins = mm3(ps[:, :], hTh[:, k, ts], hTl[:, k, ts], wh[:, k, ms], wl[:, k, ms],
                                          j == 0 and k == 0, j == NB - 1 and k == 1)
                            if j == NB - 1:
                                done(ins, label)
                    if j < NB - 1:
                        ins.then_inc(unit_used, 1)
                    if j == NB - 1:
                        norm_T("mix", 1)
                hb = j // 2 if (kind == "gu" and j == 1) else j + 1 if (kind == "down" and j < NB - 1) else None
                if hb is not None:
                    label = ("hT", L, hb)
                    ps = claim(label)
                    for t in range(NT):
                        pe.wait_ge(h_ready, 2 * hb + t + 1)
                        for c in range(2):
                            ins = te.transpose(ps[:, c * S + t * P:c * S + t * P + P], hh[:, t, c * P:c * P + P],
                                               ident[:, :])
                    done(ins, label)
                if (kind, j) == ("q", 3):
                    pe.wait_ge(kT_ready, 4 * L + 4)
                    pe.wait_ge(qT_ready, 4 * L + 4)
                    for b in range(4):
                        t, hp = divmod(b, 2)
                        ps = claim(("score", L, b))
                        for hl in range(2):
                            h = 2 * hp + hl
                            for k in range(2):
                                ins = te.matmul(ps[:, hl * S:hl * S + S], qT[:, 2 * h + k, t * P:t * P + P],
                                                kT[:, 2 * h + k, :], start=(k == 0), stop=(k == 1))
                        done(ins, ("score", L, b))
                if (kind, j) == ("v", 3):
                    pe.wait_ge(p_norm, 8 * L + 8)
                    for h in range(NH):
                        ps = claim(("pT", L, h))
                        for mc in range(2):
                            for t in range(NT):
                                i = 4 * t + h
                                ins = te.transpose(ps[:, mc * S + t * P:mc * S + t * P + P],
                                                   prob[:, i, mc * P:mc * P + P], ident[:, :])
                        done(ins, ("pT", L, h))
                    pe.wait_ge(v_ready, 4 * L + 4)
                    for h in range(NH):
                        pe.wait_ge(pT_ready, 4 * L + h + 1)
                        ps = claim(("pv", L, h))
                        for dd in range(2):
                            for mc in range(2):
                                ins = te.matmul(ps[:, dd * S:dd * S + S],
                                                v_sb[:, mc, h * HD + dd * P:h * HD + dd * P + P],
                                                pT[:, 2 * h + mc, :], start=(mc == 0), stop=(mc == 1))
                        done(ins, ("pv", L, h))

            N = norm_id("ffn", 1)
            ps = claim(("logitsT",))

            def logits_T(chunks):
                for k in chunks:
                    pe.wait_ge(ht_lo, 4 * N + k // 2 + 1)
                    ins = mm3(ps[0:NE, 0:S], wrh[:, k, :], wrl[:, k, :], XH[:, k, :], XL[:, k, :], k == 0,
                              k == KC - 1)
                return ins

            pe.wait_ge(wr_lo, 1)
            logits_T(range(4))
            x_T("ffn", 1, "xo", 1)
            done(logits_T(range(4, KC)), ("logitsT",))
            ps = claim(("logits",))
            pe.wait_ge(lgT_ready, 1)
            for t in range(NT):
                ins = te.transpose(ps[:, t * NE:t * NE + NE], lgT[:, t * P:t * P + P], ident[0:NE, 0:NE])
            done(ins, ("logits",))
            pe.wait_ge(sel_ready, 5)
            ps = claim(("rank",))
            te.matmul(ps[:, 0:NE], upper[:, :], SEL[:, 0, :], start=True, stop=True)
            te.matmul(ps[:, NE:2 * NE], ones[:, :], SEL[:, 0, :], start=True, stop=False)
            done(te.matmul(ps[:, NE:2 * NE], upper[:, :], SEL[:, 1, :], start=False, stop=True), ("rank",))
            ps = claim(("count",))
            te.matmul(ps[:, 0:NE], ones[:, :], SEL[:, 0, :], start=True, stop=False)
            done(te.matmul(ps[:, 0:NE], ones[:, :], SEL[:, 1, :], start=False, stop=True), ("count",))

            def gather(b, first=False):
                for c in range(2):
                    k = 2 * b + c
                    o = bank[GATHER_BANK[b]][:, c * 2 * P:c * 2 * P + 2 * P].rearrange("p (a s) -> p a s", a=2)
                    for i, (src, t) in enumerate(((xnh, 0), (xnh, 1), (xnl, 0), (xnl, 1))):
                        if first and b == 0 and c == 0 and i >= 2:
                            pe.wait_ge(xnl_ready, t + 1)
                        ins = te.matmul(o, src[:, t, k * P:k * P + P],
                                        PMr[:, t, :].unsqueeze(1).to_broadcast([P, 2, P]), start=(i == 0),
                                        stop=(i == 3))
                ins.then_inc(bank_full[GATHER_BANK[b]], 1)

            pe.wait_ge(xnh_ready, NT)
            pe.wait_ge(PMr_ready, 1)
            for b in range(4):
                claim(("gather", b))
                gather(b, True)
            pe.wait_ge(nit_ready, 1)
            for b in (2, 3, 4, 7):
                pe.wait_ge(*read(plan.last[b]))
            n = pe.value_load(n_it[0:1, 0:1], min_val=NE, max_val=2 * NE)
            with pe.Fori(0, n) as it:
                def claim_m(label):
                    prev = per.before[label]
                    back = prev is None
                    pe.wait_ge(*mread(prev or per.last[per.of[label][0]], back, it))
                    return bank[per.of[label][0]]

                def done_m(ins, label):
                    ins.then_inc(bank_full[per.of[label][0]], 1)

                def hT_m(b):
                    pe.wait_ge(h_ready, it * NB + (2 * NB + b + 1))
                    ps = claim_m(("hT", b))
                    for c in range(2):
                        ins = te.transpose(ps[:, c * P:c * P + P], hh[:, 0, c * P:c * P + P], ident[:, :])
                    done_m(ins, ("hT", b))

                for i, (kind, j) in enumerate(moe):
                    if kind == "gu" and j == 0:
                        pe.wait_ge(g_lo, it * 4 + 4)
                    if kind == "down":
                        pe.wait_ge(hT_lo, it * NB + (NB + j + 1))
                    pe.wait_ge(lo_ready, it * NM + (NA + i + 1))
                    wh, wl = WH[:, (NA + i) % HL, :], WL[:, (NA + i) % HL, :]
                    if kind == "gu":
                        b = j // 2
                        wh = wh.rearrange("p (k n) -> p k n", k=4)
                        wl = wl.rearrange("p (k n) -> p k n", k=4)
                        ps = claim_m(("gu", b)) if j % 2 == 0 else bank[b % 2]
                        for k in range(4):
                            kk = 4 * (j % 2) + k
                            ins = mm3(ps[:, :], XH[:, kk, 0:P], XL[:, kk, 0:P], wh[:, k, :], wl[:, k, :],
                                      kk == 0, kk == KC - 1)
                        if j % 2:
                            done_m(ins, ("gu", b))
                        else:
                            ins.then_inc(unit_used, 1)
                    else:
                        wh = wh.rearrange("p (k n) -> p k n", k=2)
                        wl = wl.rearrange("p (k n) -> p k n", k=2)
                        for m in range(2):
                            ps = claim_m(("y", m)) if j == 0 else bank[3 + m]
                            ms = slice(m * 512, m * 512 + 512)
                            for k in range(2):
                                ks = slice(k * P, k * P + P)
                                ins = mm3(ps[:, :], hTh[:, 0, ks], hTl[:, 0, ks], wh[:, k, ms], wl[:, k, ms],
                                          j == 0 and k == 0, j == NB - 1 and k == 1)
                            if j == NB - 1:
                                done_m(ins, ("y", m))
                        if j < NB - 1:
                            ins.then_inc(unit_used, 1)
                    if kind == "gu" and j == 2:
                        ps = claim_m(("PT",))
                        for t in range(NT):
                            ins = te.transpose(ps[:, t * P:t * P + P], PM[:, t, :], ident[:, :])
                        done_m(ins, ("PT",))
                    if kind == "gu" and j % 2 == 0 and j:
                        hT_m(j // 2 - 1)
                    if kind == "down" and j == NB - 2:
                        hT_m(NB - 1)
                        pe.wait_ge(PMr_ready, it + 2)
                        for b in range(2):
                            claim_m(("gather", b))
                            gather(b)
                for b in (2, 3):
                    claim_m(("gather", b))
                    gather(b)
                pe.wait_ge(PT_ready, it + 1)
                for r in range(4):
                    m, t = divmod(r, 2)
                    pe.wait_ge(y_lo, it * 2 + (2 + m + 1))
                    ps = claim_m(("scatter", r))
                    ts = slice(t * P, t * P + P)
                    te.matmul(ps[:, :], PT[:, ts], yh[:, m, :], start=True, stop=False)
                    done_m(te.matmul(ps[:, :], PT[:, ts], yl[:, m, :], start=False, stop=True), ("scatter", r))


_INS = ["x", "mem", "g_mix", "w_in", "w_pool", "pool_scale", "w_dw", "b_dw", "conv_ln_g", "conv_ln_b",
        "w_conv_out", "w_mix_out", "g_xattn", "g_mem", "w_xq", "w_xkv", "w_xo", "g_ffn", "w_ffn_gu",
        "w_ffn_down", "w_router", "b_router", "w_moe_gu", "w_moe_down", "g_final"]


def kernel(**inputs):
    import numpy as np
    import concourse.bacc as bacc
    from concourse.bass_utils import run_bass_kernel_spmd

    nc = bacc.Bacc("TRN2", target_bir_lowering=False, num_devices=1)
    arrays, args = {}, []
    for name in _INS:
        a = np.ascontiguousarray(inputs[name])
        arrays[f"in_{name}"] = a
        args.append(nc.dram_tensor(f"in_{name}", a.shape, mybir.dt.from_np(a.dtype), kind="ExternalInput").ap())
    out = nc.dram_tensor("out", inputs["x"].shape, F32, kind="ExternalOutput").ap()
    trunk(nc, *args, out)
    r = run_bass_kernel_spmd(nc, [arrays], core_ids=[0])
    return r.results[0]["out"]
```
